# Optimizing a Trainium2 kernel written in Bass

```python
import math
import jax, jax.numpy as jnp
from jax import lax
import numpy as np

D_MODEL = 2048
BATCH = 1
SEQ = 256
DEPTH = 2
DEC_BATCH = 8
DEC_SEQ = 8
PAST_LEN = 2048
PAGE_SIZE = 128

N_MIXERS = 2
N_CONV_LAYERS = (DEPTH + 1) // 2
N_MLSTM_LAYERS = DEPTH // 2
CONV_WIDTH = 31
CONV_STATE = CONV_WIDTH - 1
N_HEADS = 8
DV_HEAD = D_MODEL // N_HEADS
DQK_HEAD = DV_HEAD // 2
CHUNK = 64
D_FF = -(-8 * D_MODEL // (3 * 256)) * 256
RMS_EPS = 1e-6
LN_EPS = 1e-5

kernel_name = 'hybrid_conformer_conv_mlstm_decoder_step'

def _dense(x, w):
    return jnp.einsum('btd,de->bte', x, w)

def rms_norm(x, g):
    xf = x.astype(jnp.float32)
    y = xf * lax.rsqrt(jnp.mean(xf * xf, axis=-1, keepdims=True) + RMS_EPS)
    return (y * g.astype(jnp.float32)).astype(x.dtype)

def layer_norm(x, g, b):
    xf = x.astype(jnp.float32)
    xc = xf - jnp.mean(xf, axis=-1, keepdims=True)
    var = jnp.mean(xc * xc, axis=-1, keepdims=True)
    y = xc * lax.rsqrt(var + LN_EPS) * g.astype(jnp.float32) + b.astype(jnp.float32)
    return y.astype(x.dtype)

def conv_mixer(x, past_u, w_pw1, b_pw1, w_dw, b_dw, ln_g, ln_b, w_pw2, b_pw2):
    a, g = jnp.split(_dense(x, w_pw1) + b_pw1, 2, axis=-1)
    u = a * jax.nn.sigmoid(g)
    u_full = jnp.concatenate([past_u.astype(u.dtype), u], axis=1)
    y = lax.conv_general_dilated(
        u_full, w_dw[:, None, :], window_strides=(1,), padding='VALID',
        dimension_numbers=('NWC', 'WIO', 'NWC'), feature_group_count=D_MODEL) + b_dw
    y = jax.nn.silu(layer_norm(y, ln_g, ln_b))
    out = _dense(y, w_pw2) + b_pw2
    return out, u_full[:, -CONV_STATE:]

def mlstm_cell(q, k, v, log_i, log_f, C0, n0, m0):
    B, T = q.shape[0], q.shape[1]
    L = math.gcd(T, CHUNK)
    nc = T // L

    def to_chunks(a):
        a = a.reshape((B, nc, L) + a.shape[2:])
        return jnp.swapaxes(jnp.moveaxis(a, 1, 0), 2, 3)

    causal = jnp.tril(jnp.ones((L, L), dtype=bool))

    def step(carry, inp):
        C, n, m = carry
        qb, kb, vb, ib, fb = inp
        b = jnp.cumsum(fb, axis=-1)
        a_inter = b + m[..., None]
        d_intra = b[..., :, None] - b[..., None, :] + ib[..., None, :]
        d_intra = jnp.where(causal, d_intra, -jnp.inf)
        m_t = jnp.maximum(a_inter, jnp.max(d_intra, axis=-1))
        w_inter = jnp.exp(a_inter - m_t)
        s = jnp.einsum('bhtk,bhsk->bhts', qb, kb) * jnp.exp(d_intra - m_t[..., None])
        num = (w_inter[..., None] * jnp.einsum('bhtk,bhkv->bhtv', qb, C)
               + jnp.einsum('bhts,bhsv->bhtv', s, vb))
        den = w_inter * jnp.einsum('bhtk,bhk->bht', qb, n) + jnp.sum(s, axis=-1)
        h = num / jnp.maximum(jnp.abs(den), jnp.exp(-m_t))[..., None]
        m_new = m_t[..., -1]
        g_state = jnp.exp(b[..., -1] + m - m_new)
        g_rows = jnp.exp(b[..., -1:] - b + ib - m_new[..., None])
        kw = kb * g_rows[..., None]
        C_new = g_state[..., None, None] * C + jnp.einsum('bhsk,bhsv->bhkv', kw, vb)
        n_new = g_state[..., None] * n + jnp.sum(kw, axis=2)
        return (C_new, n_new, m_new), h

    (C, n, m), hs = lax.scan(step, (C0, n0, m0), tuple(map(to_chunks, (q, k, v, log_i, log_f))))
    h = jnp.moveaxis(jnp.swapaxes(hs, 2, 3), 0, 1).reshape(B, T, N_HEADS, DV_HEAD)
    return h, C, n, m

def mlstm_mixer(x, C0, n0, m0, w_q, w_k, w_v, w_o, w_i, b_i, w_f, b_f, g_mh, w_out):
    B, T, _ = x.shape
    f32 = jnp.float32
    q = _dense(x, w_q).reshape(B, T, N_HEADS, DQK_HEAD).astype(f32) * (DQK_HEAD ** -0.5)
    k = _dense(x, w_k).reshape(B, T, N_HEADS, DQK_HEAD).astype(f32)
    v = _dense(x, w_v).reshape(B, T, N_HEADS, DV_HEAD).astype(f32)
    log_i = (_dense(x, w_i) + b_i).astype(f32)
    log_f = jax.nn.log_sigmoid((_dense(x, w_f) + b_f).astype(f32))
    o = jax.nn.sigmoid(_dense(x, w_o))
    h, C, n, m = mlstm_cell(q, k, v, log_i, log_f,
                            C0.astype(f32), n0.astype(f32), m0.astype(f32))
    h = h * lax.rsqrt(jnp.mean(h * h, axis=-1, keepdims=True) + RMS_EPS)
    h = h.reshape(B, T, D_MODEL) * g_mh.astype(f32)
    out = _dense(o * h.astype(x.dtype), w_out)
    return out, C.astype(C0.dtype), n.astype(n0.dtype), m.astype(m0.dtype)

def swiglu_ffn(x, w_gate, w_up, w_down):
    return _dense(jax.nn.silu(_dense(x, w_gate)) * _dense(x, w_up), w_down)

def setup_inputs(seed: int = 0) -> dict:
    key = jax.random.key(seed)
    ks = iter(jax.random.split(key, 40))

    def nrm(shape, scale):
        return scale * jax.random.normal(next(ks), shape, jnp.float32)

    D = D_MODEL
    NC, NM = N_CONV_LAYERS, N_MLSTM_LAYERS
    HK = N_HEADS * DQK_HEAD
    HV = N_HEADS * DV_HEAD
    return {
        'x_prompt': nrm((BATCH, SEQ, D), 1.0),
        'x_sample': nrm((DEC_BATCH, DEC_SEQ, D), 1.0),
        'cache_conv': nrm((NC, DEC_BATCH, CONV_STATE, D), 0.5),
        'state_C': nrm((NM, DEC_BATCH, N_HEADS, DQK_HEAD, DV_HEAD), 0.3),
        'state_n': nrm((NM, DEC_BATCH, N_HEADS, DQK_HEAD), 0.3),
        'state_m': nrm((NM, DEC_BATCH, N_HEADS), 0.5),
        'conv_w_pw1': nrm((NC, D, 2 * D), D ** -0.5),
        'conv_b_pw1': nrm((NC, 2 * D), 0.02),
        'conv_w_dw': nrm((NC, CONV_WIDTH, D), CONV_WIDTH ** -0.5),
        'conv_b_dw': nrm((NC, D), 0.02),
        'conv_ln_g': 1.0 + nrm((NC, D), 0.05),
        'conv_ln_b': nrm((NC, D), 0.02),
        'conv_w_pw2': nrm((NC, D, D), D ** -0.5),
        'conv_b_pw2': nrm((NC, D), 0.02),
        'mlstm_w_q': nrm((NM, D, HK), D ** -0.5),
        'mlstm_w_k': nrm((NM, D, HK), D ** -0.5),
        'mlstm_w_v': nrm((NM, D, HV), D ** -0.5),
        'mlstm_w_o': nrm((NM, D, HV), D ** -0.5),
        'mlstm_w_i': nrm((NM, D, N_HEADS), D ** -0.5),
        'mlstm_b_i': -3.0 + nrm((NM, N_HEADS), 0.1),
        'mlstm_w_f': nrm((NM, D, N_HEADS), D ** -0.5),
        'mlstm_b_f': 3.0 + nrm((NM, N_HEADS), 0.1),
        'mlstm_g_norm': 1.0 + nrm((NM, HV), 0.05),
        'mlstm_w_out': nrm((NM, HV, D), HV ** -0.5),
        'ffn_w_gate': nrm((DEPTH, D, D_FF), D ** -0.5),
        'ffn_w_up': nrm((DEPTH, D, D_FF), D ** -0.5),
        'ffn_w_down': nrm((DEPTH, D_FF, D), D_FF ** -0.5),
        'norm_mix_pre': 1.0 + nrm((DEPTH, D), 0.05),
        'norm_mix_post': 1.0 + nrm((DEPTH, D), 0.05),
        'norm_ffn_pre': 1.0 + nrm((DEPTH, D), 0.05),
        'norm_ffn_post': 1.0 + nrm((DEPTH, D), 0.05),
    }

def reference(x_prompt, x_sample, cache_conv, state_C, state_n, state_m,
              conv_w_pw1, conv_b_pw1, conv_w_dw, conv_b_dw, conv_ln_g, conv_ln_b,
              conv_w_pw2, conv_b_pw2,
              mlstm_w_q, mlstm_w_k, mlstm_w_v, mlstm_w_o, mlstm_w_i, mlstm_b_i,
              mlstm_w_f, mlstm_b_f, mlstm_g_norm, mlstm_w_out,
              ffn_w_gate, ffn_w_up, ffn_w_down,
              norm_mix_pre, norm_mix_post, norm_ffn_pre, norm_ffn_post):
    conv_zero = jnp.zeros((BATCH, CONV_STATE, D_MODEL), cache_conv.dtype)
    C_zero = jnp.zeros((BATCH, N_HEADS, DQK_HEAD, DV_HEAD), state_C.dtype)
    n_zero = jnp.zeros((BATCH, N_HEADS, DQK_HEAD), state_n.dtype)
    m_zero = jnp.zeros((BATCH, N_HEADS), state_m.dtype)

    xs = [x_prompt, x_sample]
    conv_new = [[], []]
    C_new, n_new, m_new = [[], []], [[], []], [[], []]
    for i in range(DEPTH):
        j = i // N_MIXERS
        for gi in range(2):
            x = xs[gi]
            h = rms_norm(x, norm_mix_pre[i])
            if i % N_MIXERS == 0:
                past = conv_zero if gi == 0 else cache_conv[j]
                mix, buf = conv_mixer(h, past, conv_w_pw1[j], conv_b_pw1[j], conv_w_dw[j],
                                      conv_b_dw[j], conv_ln_g[j], conv_ln_b[j],
                                      conv_w_pw2[j], conv_b_pw2[j])
                conv_new[gi].append(buf)
            else:
                if gi == 0:
                    C0, n0, m0 = C_zero, n_zero, m_zero
                else:
                    C0, n0, m0 = state_C[j], state_n[j], state_m[j]
                mix, C1, n1, m1 = mlstm_mixer(h, C0, n0, m0, mlstm_w_q[j], mlstm_w_k[j],
                                              mlstm_w_v[j], mlstm_w_o[j], mlstm_w_i[j],
                                              mlstm_b_i[j], mlstm_w_f[j], mlstm_b_f[j],
                                              mlstm_g_norm[j], mlstm_w_out[j])
                C_new[gi].append(C1)
                n_new[gi].append(n1)
                m_new[gi].append(m1)
            x = x + rms_norm(mix, norm_mix_post[i])
            f = swiglu_ffn(rms_norm(x, norm_ffn_pre[i]), ffn_w_gate[i], ffn_w_up[i], ffn_w_down[i])
            xs[gi] = x + rms_norm(f, norm_ffn_post[i])

    return (xs[0], xs[1],
            jnp.stack(conv_new[0]), jnp.stack(conv_new[1]),
            jnp.stack(C_new[0]), jnp.stack(n_new[0]), jnp.stack(m_new[0]),
            jnp.stack(C_new[1]), jnp.stack(n_new[1]), jnp.stack(m_new[1]))


_drawn_inputs = setup_inputs


def setup_inputs(seed=0):
    import zlib

    import numpy as np

    out = dict(_drawn_inputs(seed))
    spreads = {}
    factors = {}
    for name, (base, spread) in spreads.items():
        noise = np.random.default_rng([zlib.crc32(name.encode()), seed]).standard_normal(out[name].shape)
        drawn = base * np.exp(spread * noise) if base else spread * noise
        out[name] = __import__('jax').numpy.asarray(drawn.astype(out[name].dtype))
    for name, factor in factors.items():
        out[name] = (out[name] * factor).astype(out[name].dtype)
    return out
```

```python
from contextlib import ExitStack

import concourse.bass as bass
from concourse import mybir

ALU = mybir.AluOpType
ACT = mybir.ActivationFunctionType
F32 = mybir.dt.float32
F32R = mybir.dt.float32r

P = 128
BIG = -1.0e30
AHEAD = 3
SLOTS = 4
BANKS = 4


class Phase:

    def __init__(self, name, units, groups, dmas):
        self.name, self.units, self.groups, self.dmas = name, units, groups, dmas


def plan(C, FC, H):
    segs = [24, FC - 24]
    ups = lambda l: [Phase(f"up{l}a", C // 2, segs[0] // 2, 2), Phase(f"down{l}a", segs[0] // 2, C // 4, 2),
                     Phase(f"up{l}b", C // 2, segs[1] // 2, 2), Phase(f"down{l}b", segs[1] // 2, C // 4, 2)]
    order = [Phase("pw1", C // 2, C // 2, 2), Phase("pw2", C // 2, C // 4, 2), *ups(0),
             Phase("qkv", C // 2, H, 3), Phase("o", C // 2, C // 4, 3), Phase("out", C // 2, C // 4, 2), *ups(1)]
    unit = group = landed = 0
    for p in order:
        p.unit0, p.group0, p.landed0 = unit, group, landed
        unit += p.units * p.groups
        group += p.groups
        landed += p.units * p.groups // SLOTS * 16 * p.dmas
    return order, unit, segs


def trunk_kernel(
    nc: bass.Bass,
    x_prompt: bass.AP, x_sample: bass.AP, cache_conv: bass.AP, state_C: bass.AP, state_n: bass.AP,
    state_m: bass.AP, conv_w_pw1: bass.AP, conv_b_pw1: bass.AP, conv_w_dw: bass.AP,
    conv_b_dw: bass.AP, conv_ln_g: bass.AP, conv_ln_b: bass.AP, conv_w_pw2: bass.AP,
    conv_b_pw2: bass.AP, mlstm_w_q: bass.AP, mlstm_w_k: bass.AP, mlstm_w_v: bass.AP,
    mlstm_w_o: bass.AP, mlstm_w_i: bass.AP, mlstm_b_i: bass.AP, mlstm_w_f: bass.AP,
    mlstm_b_f: bass.AP, mlstm_g_norm: bass.AP, mlstm_w_out: bass.AP, ffn_w_gate: bass.AP,
    ffn_w_up: bass.AP, ffn_w_down: bass.AP, norm_mix_pre: bass.AP, norm_mix_post: bass.AP,
    norm_ffn_pre: bass.AP, norm_ffn_post: bass.AP,
    y_prompt: bass.AP, y_sample: bass.AP, conv_prompt: bass.AP, conv_sample: bass.AP,
    C_prompt: bass.AP, n_prompt: bass.AP, m_prompt: bass.AP,
    C_sample: bass.AP, n_sample: bass.AP, m_sample: bass.AP,
):
    _, TP, D = x_prompt.shape
    B, L, _ = x_sample.shape
    TS = B * L
    T = TP + TS
    C = D // P
    _, _, H, DK, DV = state_C.shape
    W = conv_w_dw.shape[1]
    TAIL = W - 1
    DFF = ffn_w_gate.shape[2]
    FC = DFF // P
    assert DK == P and DV == 2 * P and TP == 2 * P and TS <= 64 and C == 2 * H
    RMS_EPS, LN_EPS = 1e-6, 1e-5
    phases, n_units, segs = plan(C, FC, H)
    ph = {p.name: p for p in phases}
    follows = {p.name: q for p, q in zip(phases, phases[1:])}
    PREPS = ["pw1", "pw2", "up0a", "qkv", "out", "up1a", "end"]
    prep_no = {name: i for i, name in enumerate(PREPS)}
    up_first = {"up0a": 0, "up0b": segs[0] // 2, "up1a": FC // 2, "up1b": FC // 2 + segs[0] // 2}
    seg_of = {"a": 0, "b": segs[0]}
    sq_no = {"pw2": 0, "down0b": 1, "out": 2, "down1b": 3}
    sq_preps = ["pw1", "up0a", "qkv", "up1a"]
    ROOTS = [0, 2, 3, 4, 6, 7, 9, 10, 12, 13]
    LN_VAR = 3
    M_STEPS = 10

    ctx = ExitStack()
    with ctx:
        def sem(name):
            return ctx.enter_context(nc.semaphore(name))

        at = [(nc.sbuf_base + 63) // 64 * 64]

        def sb(name, shape, dt=F32, place=None):
            size = 4
            for n in shape[1:]:
                size *= n
            where = at[0] if place is None else place[0]
            nxt = (where + size + 31) // 32 * 32
            if place is None:
                at[0] = nxt
            else:
                place[0] = nxt
            return nc.alloc_sbuf_tensor_at(name, list(shape), dt, offset=where)

        x = sb("x", [P, C, T])
        xh = sb("xh", [P, C, T], F32R)
        xl = sb("xl", [P, C, T], F32R)
        branch_at = [at[0]]
        branch = sb("branch", [P, C, T])
        raw = sb("raw", [P, SLOTS, 2, 512])
        hi = sb("hi", [P, SLOTS, 2, 512], F32R)
        lo = sb("lo", [P, SLOTS, 2, 512], F32R)
        shared_at = at[0]
        hh = sb("hh", [P, segs[0], T], F32R)
        hl = sb("hl", [P, segs[0], T], F32R)
        shared_end = at[0]
        vrows = sb("vrows", [P, 2, P])
        n_wdw = W * C
        vcol = sb("vcol", [P, 2 * P + n_wdw])
        ident = sb("ident", [P, P])
        ones = sb("ones", [P, P])
        eps = sb("eps", [P, 2])
        rx = sb("rx", [P, T])
        rp = sb("rp", [P, T])
        root = sb("root", [P, T])
        sq = sb("sq", [P, 2, 2, T])
        acc = sb("acc", [P, T])
        accA = sb("accA", [P, T])
        accB = sb("accB", [P, T])
        tA = sb("tA", [P, 2, T])
        tB = sb("tB", [P, 2, T])
        w_if = sb("w_if", [P, C, 40])
        n0_rows = sb("n0_rows", [B * H, P])
        b_gate = sb("b_gate", [H, 2])
        m0 = sb("m0", [H, B])
        mask_p = sb("mask_p", [P, TP])
        mask_s = sb("mask_s", [TS, TS])
        seg = sb("seg", [TS, B])
        assert at[0] <= nc.sbuf_usable_end, at[0]

        here = [shared_at]
        u_smp = sb("u_smp", [P, C, B, TAIL + L], place=here)
        u_rows_at = here[0]
        cache_rows = sb("cache_rows", [B // 2 * TAIL, 2, D], place=here)
        u_rows = sb("u_rows", [TS, 2, D], place=[u_rows_at])
        u_prm_at = here[0]
        u_prm = sb("u_prm", [P, C, TAIL + TP], place=here)
        x_rows2 = sb("x_rows2", [TS, D], place=[u_prm_at])
        assert here[0] <= shared_end
        x_rows = sb("x_rows", [P, 2, D], place=[branch_at[0]])
        wdw_rows = sb("wdw_rows", [P, 4, P], place=here)
        u_new = sb("u_new", [P, C, TS], place=here)
        assert here[0] <= shared_end
        here = [shared_at]
        cell = lambda name, shape: sb(name, shape, place=here)
        hn = cell("hn", [P, C, T])
        qT = cell("qT", [P, T])
        kT = cell("kT", [P, T])
        vT = cell("vT", [P, 2, T])
        v_tok = cell("v_tok", [P, 3, DV])
        kw = cell("kw", [P, 3, DK])
        kw_seq = cell("kw_seq", [TS, B, DK])
        prob = cell("prob", [P, 3 * P])
        prob_s = cell("prob_s", [TS, TS])
        rows = cell("rows", [H, 2 * T + TS])
        rows_h = cell("rows_h", [H, 2 * T + TS])
        C0 = cell("C0", [P, B, DV])
        qw = cell("qw", [P, TS])
        qn = cell("qn", [P, TS])
        g_state = cell("g_state", [P, B])
        hq = cell("hq", [P, 2, T])
        Cn_prm = cell("Cn_prm", [P, DV + B + 1])
        c_tok = cell("c_tok", [P, 3, H])
        gr_tok = cell("gr_tok", [P, 3, H])
        tC = cell("tC", [P, 2, T])
        n0T = cell("n0T", [P, B * H])
        n_new = cell("n_new", [P, B * H + H])
        assert here[0] <= shared_end, (here[0], shared_end)
        here = [shared_at]
        row = lambda name, n=T: sb(name, [H, n], place=here)
        i_row, f_row, f_abs, f_min, b_row, c_row, d_row, keep_row, cut_row, gr_row, m_row, cum_row = (
            row(n) for n in ("i_row", "f_row", "f_abs", "f_min", "b_row", "c_row", "d_row",
                             "keep_row", "cut_row", "gr_row", "m_row", "cum_row"))
        assert here[0] <= shared_at + C * T * 4
        here = [shared_at]
        y_rows = sb("y_rows", [P, 3, D], place=here)
        PS = ctx.enter_context(nc.psum_tensor("PS", [P, 8, 512], F32))

        v_at = {}
        vec_dmas = []
        for k, (name, ap) in enumerate((("mix_pre", norm_mix_pre), ("mix_post", norm_mix_post),
                                        ("ffn_pre", norm_ffn_pre), ("ffn_post", norm_ffn_post))):
            for l in range(2):
                v_at[f"{name}{l}"] = 2 * C * k + C * l
            vec_dmas.append((2 * C * k, 2 * C, 0, ap.rearrange("l (c p) -> (l c) p", p=P)))
        r0 = 0
        for name, ap, n in (("b_pw1", conv_b_pw1, 2 * C), ("b_dw", conv_b_dw, C), ("ln_g", conv_ln_g, C),
                            ("ln_b", conv_ln_b, C), ("b_pw2", conv_b_pw2, C), ("g_mh", mlstm_g_norm, C)):
            v_at[name] = P + r0
            vec_dmas.append((r0, n, 1, ap.rearrange("l (c p) -> (l c) p", p=P)))
            r0 += n
        vec_rows = [P, r0]
        v_at["w_dw"] = 2 * P

        def vec(name, c, n=1):
            return vcol[:, bass.ds(c + v_at[name], n)]

        raw_in = [sem(f"raw_in{s}") for s in range(SLOTS)]
        hi_done, lo_done, units_used = sem("hi_done"), sem("lo_done"), sem("units_used")
        bank_done = sem("bank_done")
        banks_read = sem("banks_read")
        x_in, vec_in, cache_in, gates_in, C0_in = (sem(n) for n in ("x_in", "vec_in", "cache_in", "gates_in", "C0_in"))
        consts_ready, vec_turned, vec_ready = sem("consts_ready"), sem("vec_turned"), sem("vec_ready")
        x_turned, cache_turned, cache_ready = sem("x_turned"), sem("cache_turned"), sem("cache_ready")
        prep_scaled, prep_front, prep_act = sem("prep_scaled"), sem("prep_front"), sem("prep_act")
        prep_sq, prep_hi, prep_lo, prep_sum = sem("prep_sq"), sem("prep_hi"), sem("prep_lo"), sem("prep_sum")
        stat_sum, stat_root, stat_inv, ln_step = sem("stat_sum"), sem("stat_root"), sem("stat_inv"), sem("ln_step")
        sums_clear = sem("sums_clear")
        br_out, br_sq, br_acc = sem("br_out"), sem("br_sq"), sem("br_acc")
        up_gate, up_silu, up_prod, up_hi, h_ready = (sem(n) for n in ("up_gate", "up_silu", "up_prod", "up_hi", "h_ready"))
        glu_in, glu_sig, glu_out, conv_step, conv_sq, conv_sum = (
            sem(n) for n in ("glu_in", "glu_sig", "glu_out", "conv_step", "conv_sq", "conv_sum"))
        u_packed, u_turned, u_copied, u_out = sem("u_packed"), sem("u_turned"), sem("u_copied"), sem("u_out")
        gate_mm, row_dve, row_act, row_turned, row_cols, n0_turned = (
            sem(n) for n in ("gate_mm", "row_dve", "row_act", "row_turned", "row_cols", "n0_turned"))
        masks_ready, w_if_ready = sem("masks_ready"), sem("w_if_ready")
        head_rows, tables, scores, kv_turned = sem("head_rows"), sem("tables"), sem("scores"), sem("kv_turned")
        decay_in, decay_exp, qw_ready, qn_ready = sem("decay_in"), sem("decay_exp"), sem("qw_ready"), sem("qn_ready")
        kw_ready, kw_seq_ready, v_ready, prob_ready = sem("kw_ready"), sem("kw_seq_ready"), sem("v_ready"), sem("prob_ready")
        den_done, den_abs, den_max, den_inv, num_done = (sem(n) for n in ("den_done", "den_abs", "den_max", "den_inv", "num_done"))
        hq_ready, hq_sq, hq_sum, hq_ln, hq_rs, hn_ready = (
            sem(n) for n in ("hq_ready", "hq_sq", "hq_sum", "hq_ln", "hq_rs", "hn_ready"))
        Cp_done, Cp_read, Cs_done, C_new, n_scaled, n_done = (
            sem(n) for n in ("Cp_done", "Cp_read", "Cs_done", "C_new", "n_scaled", "n_done"))
        o_exp, o_plus, o_gate = sem("o_exp"), sem("o_plus"), sem("o_gate")
        C_out, Cp_out, m_out, n_turned, n_copied, y_turned, y_copied, stored = (
            sem(n) for n in ("C_out", "Cp_out", "m_out", "n_turned", "n_copied", "y_turned", "y_copied", "stored"))

        def landed(phase, k, s):
            return phase.landed0 + 16 * phase.dmas * (k + 1)

        def bank_of(group):
            return (group % 2) * BANKS

        def wait_bank(eng, p, g, m):
            if m < BANKS - 1:
                eng.wait_ge(bank_done, g * 3 + (3 * p.group0 + m + 1))
            else:
                eng.wait_ge(units_used, g * p.units + (p.unit0 + p.units))

        def acc_count(p, g, m):
            return g * BANKS + (sq_no[p.name] * (C + 1) + 1 + m)

        def out_count(p, g):
            return g * 3 + sq_no[p.name] * 3 * (C // BANKS)

        def weight_dmas(p, g, j, slot):
            pair = lambda ap: ap.rearrange("(k p) n -> p k n", p=P)
            rows2 = lambda w, first: pair(w)[:, first:first + 2, :]
            half = BANKS // 2 * P
            if p.name == "pw1":
                w = rows2(conv_w_pw1[0], 2 * j)
                yield raw[:, slot, :, 0:half], w[:, :, bass.ds(g * half, half)]
                yield raw[:, slot, :, half:2 * half], w[:, :, bass.ds(g * half + D, half)]
            elif p.name[:2] == "up":
                l, s0 = int(p.name[2]), seg_of[p.name[3]] * P
                yield raw[:, slot, :, 0:half], rows2(ffn_w_gate[l], 2 * j)[:, :, bass.ds(g * half + s0, half)]
                yield raw[:, slot, :, half:2 * half], rows2(ffn_w_up[l], 2 * j)[:, :, bass.ds(g * half + s0, half)]
            elif p.name == "qkv":
                yield raw[:, slot, :, 0:P], rows2(mlstm_w_q[0], 2 * j)[:, :, bass.ds(g * P, P)]
                yield raw[:, slot, :, P:2 * P], rows2(mlstm_w_k[0], 2 * j)[:, :, bass.ds(g * P, P)]
                yield raw[:, slot, :, 2 * P:4 * P], rows2(mlstm_w_v[0], 2 * j)[:, :, bass.ds(g * DV, DV)]
            else:
                w, first = {"pw2": (conv_w_pw2[0], 0), "o": (mlstm_w_o[0], 0), "out": (mlstm_w_out[0], 0)}.get(
                    p.name) or (ffn_w_down[int(p.name[4])], seg_of[p.name[5]])
                w = rows2(w, first + 2 * j)[:, :, bass.ds(g * 512, 512)]
                yield raw[:, slot, 0, :], w[:, 0, :]
                if p.dmas == 2:
                    yield raw[:, slot, 1, :], w[:, 1, :]
                else:
                    yield raw[:, slot, 1, 0:256], w[:, 1, 0:256]
                    yield raw[:, slot, 1, 256:512], w[:, 1, 256:512]

        block = ctx.enter_context(nc.Block())

        @block.sync
        def _(sp):
            for t in range(2):
                sp.dma_start(x_rows[:, t, :], x_prompt[0, t * P:(t + 1) * P, :]).then_inc(x_in, 16)
            sp.dma_start(x_rows2[:, :], x_sample.rearrange("b t d -> (b t) d")).then_inc(x_in, 16)

            def load(p, g, j, k_in_phase, n):
                slot = j % SLOTS if p.units % SLOTS == 0 else k_in_phase % SLOTS
                if p.unit0 or not isinstance(n, int) or n >= SLOTS:
                    sp.wait_ge(lo_done, n - (SLOTS - 1))
                for dst, src in weight_dmas(p, g, j, slot):
                    sp.dma_start(dst, src).then_inc(raw_in[slot], 16)

            for p in phases:
                per = 1 if p.units % SLOTS == 0 else 2
                first = 0
                if p.unit0 == 0:
                    for j in range(p.units):
                        load(p, 0, j, j, j)
                    first = 1
                with sp.Fori(first, p.groups // per) as it:
                    for r in range(per):
                        for j in range(p.units):
                            load(p, it * per + r, j, r * p.units + j, it * (per * p.units) + (p.unit0 + r * p.units + j))

        @block.gpsimd
        def _(pool):
            g = nc.gpsimd
            for r, n, k, src in vec_dmas:
                pool.dma_start(vrows[r:r + n, k, :], src).then_inc(vec_in, 16)
            wdw = conv_w_dw[0].rearrange("j (c p) -> (j c) p", p=P)
            for k in range(4):
                n = min(P, n_wdw - k * P)
                pool.dma_start(wdw_rows[0:n, k, :], wdw[k * P:k * P + n, :]).then_inc(vec_in, 16)
            g.memset(ident[:, :], 0.0).then_inc(consts_ready, 1)
            pool.wait_ge(consts_ready, 1)
            g.affine_select(out=ident[:, :], in_=ident[:, :], compare_op=ALU.not_equal, fill=1.0, base=0,
                            pattern=[[-1, P]], channel_multiplier=1).then_inc(consts_ready, 1)
            g.memset(ones[:, :], 1.0).then_inc(consts_ready, 1)
            g.memset(eps[:, 0:1], RMS_EPS).then_inc(consts_ready, 1)
            g.memset(eps[:, 1:2], LN_EPS).then_inc(consts_ready, 1)
            pool.dma_start(cache_rows[:, :, :], cache_conv[0].rearrange("(r b) t d -> (b t) r d", r=2)).then_inc(cache_in, 16)
            pool.dma_start(conv_sample[0, :, 0:TAIL - L, :], cache_conv[0, :, L:TAIL, :]).then_inc(stored, 16)

            def clear_sums(k, *sums):
                for s in sums:
                    last = g.memset(s[:, :], 0.0)
                last.then_inc(sums_clear, 1)
                pool.wait_ge(sums_clear, k)

            def sum_prep(name, k_clear):
                q0 = C // 2 * sq_preps.index(name)
                if k_clear > 2:
                    pool.wait_ge(prep_sum, 2 * q0)
                    pool.wait_ge(stat_root, ROOTS[2 * k_clear - 2])
                clear_sums(k_clear, accA)
                for j in range(C // 2):
                    pool.wait_ge(prep_sq, q0 + j + 1)
                    for i in range(2):
                        k = 2 * (q0 + j) + i
                        if i or j:
                            pool.wait_ge(prep_sum, k)
                        g.tensor_tensor(accA[:, :], accA[:, :], sq[:, j % 2, i, :], ALU.add).then_inc(prep_sum, 1)

            sum_prep("pw1", 1)
            g.memset(w_if[:, :, :], 0.0).then_inc(w_if_ready, 1)
            pool.wait_ge(w_if_ready, 1)
            with nc.allow_non_contiguous_dma(reason="gate weights and states of a few bytes a row"):
                pool.dma_start(w_if[:, :, 0:H], mlstm_w_i[0].rearrange("(c p) h -> p c h", p=P)).then_inc(gates_in, 16)
                pool.dma_start(w_if[:, :, 32:32 + H], mlstm_w_f[0].rearrange("(c p) h -> p c h", p=P)).then_inc(gates_in, 16)
                pool.dma_start(b_gate[:, 0:1], mlstm_b_i.rearrange("l h -> h l")).then_inc(gates_in, 16)
                pool.dma_start(b_gate[:, 1:2], mlstm_b_f.rearrange("l h -> h l")).then_inc(gates_in, 16)
                pool.dma_start(m0[:, :], state_m[0].rearrange("b h -> h b")).then_inc(gates_in, 16)
            pool.dma_start(n0_rows[:, :], state_n[0].rearrange("b h k -> (b h) k")).then_inc(gates_in, 16)
            g.memset(mask_p[:, :], 0.0)
            g.memset(mask_s[:, :], 0.0)
            g.memset(seg[:, :], 1.0).then_inc(masks_ready, 1)
            pool.wait_ge(masks_ready, 1)
            g.affine_select(out=mask_p[:, :], in_=mask_p[:, :], compare_op=ALU.is_ge, fill=BIG, base=0,
                            pattern=[[1, TP]], channel_multiplier=-1)
            g.affine_select(out=mask_s[:, :], in_=mask_s[:, :], compare_op=ALU.is_ge, fill=BIG, base=0,
                            pattern=[[1, TS]], channel_multiplier=-1)
            g.affine_select(out=seg[:, :], in_=seg[:, :], compare_op=ALU.is_ge, fill=0.0, base=0,
                            pattern=[[-L, B]], channel_multiplier=1).then_inc(masks_ready, 1)
            pool.wait_ge(masks_ready, 2)
            g.affine_select(out=mask_s[:, :], in_=mask_s[:, :], compare_op=ALU.is_ge, fill=BIG, base=0,
                            pattern=[[-L, B], [0, L]], channel_multiplier=1)
            last = g.affine_select(out=seg[:, :], in_=seg[:, :], compare_op=ALU.is_ge, fill=0.0, base=L - 1,
                                   pattern=[[L, B]], channel_multiplier=-1)
            last.then_inc(masks_ready, 1)
            pool.wait_ge(stat_root, 2)
            g.memset(accA[:, :], 0.0).then_inc(conv_sum, 1)
            g.memset(accB[:, :], 0.0).then_inc(conv_sum, 1)
            with pool.Fori(0, C) as c:
                pool.wait_ge(conv_sq, c + 1)
                pool.wait_ge(conv_sum, c * 2 + 2)
                g.tensor_tensor(accA[:, :], accA[:, :], branch[:, c, :], ALU.add).then_inc(conv_sum, 1)
                g.tensor_tensor(accB[:, :], accB[:, :], sq[:, 0, c % 2, :], ALU.add).then_inc(conv_sum, 1)

            pool.wait_ge(u_copied, 2 * C // 4)
            for b in range(B):
                pool.dma_start(conv_sample[0, b, TAIL - L:TAIL, :], u_rows[b * L:(b + 1) * L, 0, :]).then_inc(u_out, 16)
            pool.dma_start(conv_prompt[0, 0, :, :], u_rows[0:TAIL, 1, :]).then_inc(u_out, 16)

            pool.wait_ge(ln_step, 1)
            sum_prep("up0a", 2)
            sum_prep("qkv", 3)
            pool.dma_start(C0[:, :, :], state_C[0, :, 0, :, :].rearrange("b k v -> k b v")).then_inc(C0_in, 16)
            g.memset(keep_row[:, :], 1.0)
            g.memset(cut_row[:, :], 0.0).then_inc(masks_ready, 1)
            pool.wait_ge(masks_ready, 4)
            g.memset(keep_row[:, 0:1], 0.0)
            g.memset(keep_row[:, TP:T:L], 0.0)
            g.memset(cut_row[:, 0:1], BIG)
            g.memset(cut_row[:, TP:T:L], BIG).then_inc(masks_ready, 1)

            pool.wait_ge(row_dve, M_STEPS)
            with nc.allow_non_contiguous_dma(reason="64 stabilisers"):
                pool.dma_start(m_prompt.rearrange("l b h -> h (l b)"), m_row[:, TP - 1:TP]).then_inc(m_out, 16)
                pool.dma_start(m_sample[0].rearrange("b h -> h b"), m_row[:, TP + L - 1:T:L]).then_inc(m_out, 16)

            def states(h, last):
                pool.wait_ge(C_new, h * B + B)
                pool.wait_ge(Cp_read, h + 1)
                pool.dma_start(C_prompt[0, 0, bass.ds(h, 1), :, :].rearrange("h k v -> k (h v)"), Cn_prm[:, 0:DV]).then_inc(Cp_out, 16)
                pool.dma_start(C_sample[0, :, bass.ds(h, 1), :, :].rearrange("b h k v -> k (b h) v"), C0[:, :, :]).then_inc(C_out, 16)
                pool.wait_ge(C_out, h * 16 + 16)
                if not last:
                    pool.dma_start(C0[:, :, :], state_C[0, :, bass.ds(h + 1, 1), :, :].rearrange("b h k v -> k (b h) v")).then_inc(C0_in, 16)

            with pool.Fori(0, H - 1) as h:
                states(h, False)
            states(H - 1, True)
            sum_prep("up1a", 4)

            pool.wait_ge(n_copied, 1)
            pool.dma_start(n_sample[0].rearrange("b h k -> (b h) k"), vrows[0:B * H, 0, :]).then_inc(stored, 16)
            pool.dma_start(n_prompt[0].rearrange("b h k -> (b h) k"), vrows[B * H:B * H + H, 0, :]).then_inc(stored, 16)
            pool.wait_ge(Cp_out, 16 * H)
            pool.wait_ge(C_out, 16 * H)
            pool.wait_ge(m_out, 32)
            for k in range(C // 4):
                cols = slice(512 * k, 512 * (k + 1))
                pool.wait_ge(y_copied, 3 * (k + 1))
                for t in range(2):
                    pool.dma_start(y_prompt[0, t * P:(t + 1) * P, cols], y_rows[:, t, cols]).then_inc(stored, 16)
                pool.dma_start(y_sample.rearrange("b t d -> (b t) d")[:, cols], y_rows[0:TS, 2, cols]).then_inc(stored, 16)
            pool.wait_ge(u_out, 16 * (B + 1))
            pool.wait_ge(stored, 16 * (3 + 3 * (C // 4)))

        def window(p, w, split, before):
            fixed = isinstance(w, int)
            for j in range(p.units):
                for f in before.get(j, []):
                    f()
                k = j + AHEAD
                if fixed:
                    u = w * p.units + k
                    q, r = p, u
                    if u >= p.units * p.groups:
                        if p.name not in follows:
                            continue
                        q, r = follows[p.name], u - p.units * p.groups
                    split(q, r // SLOTS, (q.unit0 + r) % SLOTS, q.unit0 + r)
                else:
                    split(p, w * (p.units // SLOTS) + k // SLOTS, k % SLOTS, w * p.units + (p.unit0 + k))
            for f in before.get(p.units, []):
                f()

        @block.scalar
        def _(act):
            s = nc.scalar

            def split(p, quad, slot, n):
                act.wait_ge(raw_in[slot], landed(p, quad, slot))
                if not isinstance(n, int) or n >= SLOTS:
                    act.wait_ge(units_used, n - (SLOTS - 1))
                s.activation(hi[:, slot, :, :], raw[:, slot, :, :], ACT.Copy).then_inc(hi_done, 1)

            def stat(k, *pieces):
                act.wait_ge(stat_sum, k)
                for src, dst in pieces:
                    last = s.activation(dst, src, ACT.Sqrt, bias=eps[:, 0:1], scale=1.0 / D)
                    last.then_inc(stat_root, 1)

            def squares(p, local, group):
                b = bank_of(group)
                for m in range(BANKS):
                    chunk = local * BANKS + m
                    written = br_out if m < BANKS - 1 else banks_read
                    if p.name in ("pw2", "out"):
                        wait_bank(act, p, local, m)
                        if p.name == "pw2":
                            ins = s.activation(branch[:, chunk, :], PS[:, b + m, 0:T], ACT.Identity, bias=vec("b_pw2", chunk))
                        else:
                            ins = s.activation(branch[:, chunk, :], PS[:, b + m, 0:T], ACT.Copy)
                        ins.then_inc(written, 1)
                    act.wait_ge(written, out_count(p, local) + (m + 1) if m < BANKS - 1 else group + 1)
                    act.wait_ge(br_acc, acc_count(p, local, max(0, m - 1)))
                    s.activation(sq[:, 0, m % 2, :], branch[:, chunk, :], ACT.Square).then_inc(br_sq, 1)

            def plain_out(p, local, group):
                wait_bank(act, p, local, BANKS - 1)
                b = bank_of(group)
                s.activation(branch[:, bass.ds(local * BANKS, BANKS), :], PS[:, bass.ds(b, BANKS), 0:T],
                             ACT.Copy).then_inc(banks_read, 1)

            def up_first_half(e):
                act.wait_ge(up_gate, e + 1)
                s.activation(tA[:, :, :], tA[:, :, :], ACT.Silu).then_inc(up_silu, 1)

            def up_second_half(e, chunk):
                act.wait_ge(up_prod, e + 1)
                s.activation(hh[:, bass.ds(chunk, 2), :], tB[:, :, :], ACT.Copy).then_inc(up_hi, 1)

            def glu(local):
                act.wait_ge(glu_in, local + 1)
                for i in range(2):
                    s.activation(tB[:, i, :], tB[:, i, :], ACT.Sigmoid,
                                 bias=vec("b_pw1", local * 2 + (C + i))).then_inc(glu_sig, 1)

            def conv_squares(local):
                for i in range(2):
                    c = local * 2 + i
                    act.wait_ge(conv_step, local * (4 * W) + 4 * W)
                    act.wait_ge(conv_sum, local * 4 + 2)
                    s.activation(sq[:, 0, i, :], branch[:, c, :], ACT.Square).then_inc(conv_sq, 1)

            def prep(name, j):
                q = C // 2 * prep_no[name] + j
                if name in ("pw1", "up0a", "qkv", "up1a"):
                    layer_norm = {"pw1": "mix_pre0", "up0a": "ffn_pre0", "qkv": "mix_pre1", "up1a": "ffn_pre1"}[name]
                    act.wait_ge(prep_front, q + 1)
                    k = C // 2 * sq_preps.index(name) + j
                    if k >= 2:
                        act.wait_ge(prep_sum, 2 * k - 2)
                    s.activation(sq[:, j % 2, :, :], x[:, 2 * j:2 * j + 2, :], ACT.Square).then_inc(prep_sq, 1)
                    for c in (2 * j, 2 * j + 1):
                        last = s.activation(xh[:, c, :], x[:, c, :], ACT.Copy, scale=vec(layer_norm, c))
                    last.then_inc(prep_hi, 1)
                elif name == "pw2":
                    act.wait_ge(prep_front, q + 1)
                    for c in (2 * j, 2 * j + 1):
                        last = s.activation(branch[:, c, :], branch[:, c, :], ACT.Silu, bias=vec("ln_b", c),
                                            scale=vec("ln_g", c))
                    last.then_inc(prep_act, 1)
                    act.wait_ge(prep_act, j + 1)
                    s.activation(xh[:, 2 * j:2 * j + 2, :], branch[:, 2 * j:2 * j + 2, :], ACT.Copy).then_inc(prep_hi, 1)
                elif name == "out":
                    act.wait_ge(prep_front, q + 1)
                    s.activation(xh[:, 2 * j:2 * j + 2, :], hn[:, 2 * j:2 * j + 2, :], ACT.Copy).then_inc(prep_hi, 1)

            def preps(name, then=()):
                out = {j: [lambda j=j: prep(name, j)] for j in range(C // 2)}
                out[C // 2] = list(then)
                return out

            def stat_rx(k, group):
                b = BANKS * (group % 2)
                cut = 512 - T
                stat(k, (PS[:, b, T:512], root[:, 0:cut]), (PS[:, b + 1, T:2 * T - cut], root[:, cut:T]))

            act.wait_ge(consts_ready, 5)
            first = ph["pw1"]
            for n in range(AHEAD):
                split(first, 0, n, n)

            def cache_turn(j):
                act.wait_ge(cache_turned, j + 1)
                for i in range(2):
                    last = s.activation(u_smp[:, 2 * j + i, :, 0:TAIL], PS[:, 4 + j % 4, i * B * TAIL:(i + 1) * B * TAIL].rearrange(
                        "p (b t) -> p b t", b=B), ACT.Copy)
                last.then_inc(cache_ready, 1)

            before = preps("pw1", [lambda: stat_rx(1, 0)])
            for j in range(C // 2):
                before[j].append(lambda j=j: cache_turn(j))
            window(first, 0, split, before)
            p = first
            with act.Fori(1, p.groups - 1) as w:
                window(p, w, split, {0: [lambda: glu(w - 1)], p.units: [lambda: conv_squares(w - 1)]})
            w = p.groups - 1
            window(p, w, split, {0: [lambda: glu(w - 1)], p.units: [lambda: conv_squares(w - 1)]})

            p = ph["pw2"]

            def u_copies():
                act.wait_ge(banks_read, p.group0)
                for b in range(B):
                    last = s.activation(u_new[:, :, b * L:(b + 1) * L], u_smp[:, :, b, TAIL:TAIL + L], ACT.Copy)
                last.then_inc(u_packed, 1)
                for half in range(2):
                    for k in range(C // 4):
                        act.wait_ge(u_turned, half * (C // 4) + k + 1)
                        n = TS if half == 0 else TAIL
                        bank = (k + BANKS * (1 - half) + BANKS * (p.group0 % 2)) % 8
                        s.activation(u_rows[0:n, half, 512 * k:512 * (k + 1)], PS[0:n, bank, :], ACT.Copy).then_inc(u_copied, 1)

            def ln_root():
                act.wait_ge(ln_step, LN_VAR)
                s.activation(root[:, :], root[:, :], ACT.Sqrt, bias=eps[:, 1:2]).then_inc(stat_root, 1)

            before = preps("pw2")
            before[0] = [lambda: glu(first.groups - 1), u_copies, lambda: conv_squares(first.groups - 1), ln_root] + before[0]
            window(p, 0, split, before)
            for w in range(1, p.groups):
                window(p, w, split, {0: [lambda: squares(p, w - 1, w + (p.group0 - 1))]})

            def ffn(l, k_stat, prev):
                a, da, b, db = (ph[f"{n}{l}{s_}"] for s_ in "ab" for n in ("up", "down"))
                before = preps(f"up{l}a", [lambda: stat_rx(k_stat + 1, a.group0)])
                bank = BANKS * ((a.group0 - 1) % 2)
                before[0] = [lambda: squares(prev, prev.groups - 1, a.group0 - 1),
                             lambda: stat(k_stat, (PS[:, bank, 0:T], root[:, :]))] + before[0]
                window(a, 0, split, before)
                for up, down, start in ((a, da, 0), (b, db, 0)):
                    e0 = up_first[up.name]

                    def up_window(w):
                        return {0: [lambda: up_first_half(w + (e0 - 1))], 1: [lambda: up_second_half(w + (e0 - 1), w * 2 - 2)]}

                    if up is b:
                        window(b, 0, split, {0: [lambda: plain_out(da, da.groups - 1, da.group0 + da.groups - 1)]})
                    with act.Fori(1, up.groups - 1) as w:
                        window(up, w, split, up_window(w))
                    window(up, up.groups - 1, split, up_window(up.groups - 1))
                    window(down, 0, split, up_window(up.groups))
                    for w in range(1, down.groups):
                        f = plain_out if down is da else squares
                        window(down, w, split, {0: [lambda: f(down, w - 1, down.group0 + w - 1)]})

            act.wait_ge(u_out, 16 * (B + 1))
            ffn(0, 3, ph["pw2"])

            p = ph["qkv"]

            def row_gates():
                act.wait_ge(row_dve, 4)
                s.activation(f_abs[:, :], f_abs[:, :], ACT.Exp, scale=-1.0).then_inc(row_act, 1)
                act.wait_ge(row_act, 1)
                s.activation(f_abs[:, :], f_abs[:, :], ACT.Ln, bias=1.0).then_inc(row_act, 1)
                act.wait_ge(row_dve, M_STEPS)
                s.activation(rows[:, T + TS:2 * T + TS], m_row[:, :], ACT.Exp, scale=-1.0)
                act.wait_ge(row_dve, M_STEPS + 3)
                s.activation(rows[:, T:T + TS], rows[:, T:T + TS], ACT.Exp)
                s.activation(gr_row[:, :], gr_row[:, :], ACT.Exp).then_inc(row_act, 1)

            def cell_top(h):
                act.wait_ge(decay_in, h + 1)
                s.activation(prob[:, :], prob[:, :], ACT.Exp)
                s.activation(prob_s[:, :], prob_s[:, :], ACT.Exp).then_inc(decay_exp, 1)
                act.wait_ge(kv_turned, h + 1)
                s.activation(v_tok[:, 0:2, :], PS[:, 5, :].rearrange("p (t v) -> p t v", t=2), ACT.Copy).then_inc(v_ready, 1)

            def cell_den(h):
                act.wait_ge(den_done, h + 1)
                s.activation(root[:, :], PS[:, 6, 0:T], ACT.Abs).then_inc(den_abs, 1)
                act.wait_ge(hq_ready, h + 1)
                s.activation(sq[:, 0, :, :], hq[:, :, :], ACT.Square).then_inc(hq_sq, 1)

            def cell_norm(h):
                act.wait_ge(hq_sum, h + 1)
                s.activation(root[:, :], PS[:, 6, 0:T], ACT.Ln, bias=eps[:, 0:1], scale=1.0 / DV).then_inc(hq_ln, 1)
                act.wait_ge(hq_ln, h + 1)
                s.activation(root[:, :], root[:, :], ACT.Exp, scale=-0.5).then_inc(hq_rs, 1)
                act.wait_ge(Cp_done, h + 1)
                act.wait_ge(Cp_out, h * 16)
                act.wait_ge(n_done, h)
                s.activation(Cn_prm[:, :], PS[:, 4, 0:DV + B + 1], ACT.Copy).then_inc(Cp_read, 1)

            def cell_before(h):
                return {1: [lambda: cell_top(h)], 3: [lambda: cell_den(h)], 4: [lambda: cell_norm(h)]}

            before = preps("qkv", [lambda: stat_rx(6, p.group0), row_gates])
            bank = BANKS * ((p.group0 - 1) % 2)
            before[0] = [lambda: squares(ph["down0b"], ph["down0b"].groups - 1, p.group0 - 1),
                         lambda: stat(5, (PS[:, bank, 0:T], root[:, :]))] + before[0]
            window(p, 0, split, before)
            with act.Fori(1, p.groups) as w:
                window(p, w, split, cell_before(w - 1))
            p = ph["o"]
            window(p, 0, split, cell_before(H - 1))

            def o_exps(local):
                act.wait_ge(banks_read, ph["o"].group0 + local + 1)
                s.activation(branch[:, bass.ds(local * BANKS, BANKS), :], branch[:, bass.ds(local * BANKS, BANKS), :],
                             ACT.Exp, scale=-1.0).then_inc(o_exp, 1)

            for w in range(1, p.groups):
                window(p, w, split, {0: [lambda: o_exps(w - 1)]})
            p = ph["out"]
            before = preps("out")
            before[0] = [lambda: o_exps(C // 4 - 1)] + before[0]
            window(p, 0, split, before)
            for w in range(1, p.groups):
                window(p, w, split, {0: [lambda: squares(p, w - 1, w + (p.group0 - 1))]})
            act.wait_ge(C_out, 16 * H)
            act.wait_ge(Cp_out, 16 * H)
            ffn(1, 7, ph["out"])

            db = ph["down1b"]
            squares(db, db.groups - 1, db.group0 + db.groups - 1)
            stat(9, (PS[:, BANKS * ((db.group0 + db.groups - 1) % 2), 0:T], root[:, :]))
            for k in range(C // 4):
                for t in range(3):
                    n = P if t < 2 else TS
                    act.wait_ge(y_turned, 3 * k + t + 1)
                    s.activation(y_rows[0:n, t, 512 * k:512 * (k + 1)], PS[0:n, (3 * k + t) % 8, :], ACT.Copy).then_inc(y_copied, 1)

        @block.vector
        def _(dve):
            v = nc.vector
            done = [None]

            def split(p, quad, slot, n):
                dve.wait_ge(hi_done, n + 1)
                v.tensor_tensor(lo[:, slot, :, :], raw[:, slot, :, :], hi[:, slot, :, :].bitcast(F32),
                                ALU.subtract).then_inc(lo_done, 1)
                done[0] = n + 1

            def fence():
                dve.wait_ge(lo_done, done[0])

            def wide(t, n=2):
                return t[:, :].rearrange("p (a t) -> p a t", a=1).broadcast_to([P, n, T])

            def add_squares(p, local):
                for m in range(BANKS):
                    dve.wait_ge(br_sq, local * BANKS + (sq_no[p.name] * C + m + 1))
                    dve.wait_ge(br_acc, acc_count(p, local, m))
                    v.tensor_tensor(acc[:, :], acc[:, :], sq[:, 0, m % 2, :], ALU.add).then_inc(br_acc, 1)

            def add_branch(p, local, group):
                b = bank_of(group)
                for m in range(BANKS):
                    chunk = local * BANKS + m
                    wait_bank(dve, p, local, m)
                    v.tensor_tensor(branch[:, chunk, :], branch[:, chunk, :], PS[:, b + m, 0:T],
                                    ALU.add).then_inc(br_out if m < BANKS - 1 else banks_read, 1)
                add_squares(p, local)

            def clear_acc():
                fence()
                v.memset(acc[:, :], 0.0).then_inc(br_acc, 1)

            def inverse(k, dst, src=None):
                dve.wait_ge(stat_root, ROOTS[k])
                v.reciprocal(dst[:, :], root[:, :]).then_inc(stat_inv, 1)
                dve.wait_ge(stat_inv, k)

            def up_part1(p, local):
                b = bank_of(local + p.group0)
                wait_bank(dve, p, local, 1)
                fence()
                v.tensor_tensor(tA[:, :, :], PS[:, bass.ds(b, 2), 0:T], wide(rx), ALU.mult).then_inc(up_gate, 1)
                wait_bank(dve, p, local, 3)
                v.tensor_tensor(tB[:, :, :], PS[:, bass.ds(b + 2, 2), 0:T], wide(rx), ALU.mult).then_inc(banks_read, 1)

            def up_part2(group, e):
                dve.wait_ge(up_silu, e + 1)
                dve.wait_ge(banks_read, group + 1)
                v.tensor_tensor(tB[:, :, :], tB[:, :, :], tA[:, :, :], ALU.mult).then_inc(up_prod, 1)

            def up_part3(e, chunk):
                dve.wait_ge(up_hi, e + 1)
                v.tensor_tensor(hl[:, bass.ds(chunk, 2), :], tB[:, :, :], hh[:, bass.ds(chunk, 2), :].bitcast(F32),
                                ALU.subtract).then_inc(h_ready, 1)

            def glu_in_part(local, group):
                b = bank_of(group)
                fence()
                wait_bank(dve, ph["pw1"], local, 1)
                v.tensor_tensor(tA[:, :, :], PS[:, bass.ds(b, 2), 0:T], wide(rx), ALU.mult)
                wait_bank(dve, ph["pw1"], local, 3)
                v.tensor_tensor(tB[:, :, :], PS[:, bass.ds(b + 2, 2), 0:T], wide(rx), ALU.mult).then_inc(glu_in, 1)

            def glu_out_part(local):
                for i in range(2):
                    c = local * 2 + i
                    dve.wait_ge(glu_sig, local * 2 + (i + 1))
                    v.scalar_tensor_tensor(out=u_prm[:, c, TAIL:TAIL + TP], in0=tA[:, i, 0:TP], scalar=vec("b_pw1", c),
                                           in1=tB[:, i, 0:TP], op0=ALU.add, op1=ALU.mult)
                    last = v.scalar_tensor_tensor(
                        out=u_smp[:, c, :, TAIL:TAIL + L], in0=tA[:, i, TP:T].rearrange("p (b t) -> p b t", b=B),
                        scalar=vec("b_pw1", c), in1=tB[:, i, TP:T].rearrange("p (b t) -> p b t", b=B),
                        op0=ALU.add, op1=ALU.mult)
                last.then_inc(banks_read, 1)

            def conv_taps(local, group, taps):
                if taps[0] == 0:
                    dve.wait_ge(banks_read, group + 1)
                for j in taps:
                    for i in range(2):
                        c = local * 2 + i
                        w_j = vec("w_dw", c + j * C)
                        for part in range(2):
                            k = local * (4 * W) + (4 * j + 2 * i + part)
                            if part == 0:
                                out, u = branch[:, c, 0:TP], u_prm[:, c, j:j + TP]
                            else:
                                out = branch[:, c, TP:T].rearrange("p (b t) -> p b t", b=B)
                                u = u_smp[:, c, :, j:j + L]
                            if j == 0:
                                v.tensor_scalar(out, u, w_j, vec("b_dw", c), ALU.mult, ALU.add).then_inc(conv_step, 1)
                            else:
                                dve.wait_ge(conv_step, k - 3)
                                v.scalar_tensor_tensor(out=out, in0=u, scalar=w_j, in1=out, op0=ALU.mult,
                                                       op1=ALU.add).then_inc(conv_step, 1)

            def conv_before(local, group):
                n = ph["pw1"].units
                step = -(-W // n)
                out = {k: [lambda k=k: conv_taps(local, group, range(k * step, min(W, (k + 1) * step)))] for k in range(n)}
                out[0] = [lambda: glu_in_part(local, group), lambda: glu_out_part(local)] + out[0]
                return out

            def prep_front_part(name, j):
                q = C // 2 * prep_no[name] + j
                two = slice(2 * j, 2 * j + 2)
                if name == "pw1":
                    for c in (2 * j, 2 * j + 1):
                        dve.wait_ge(x_turned, c + 1)
                        last = v.tensor_copy(x[:, c, :], PS[:, 4 + c % 4, 0:T])
                    last.then_inc(prep_front, 1)
                elif name in ("up0a", "qkv", "up1a", "end"):
                    post = {"up0a": "mix_post0", "qkv": "ffn_post0", "up1a": "mix_post1", "end": "ffn_post1"}[name]
                    k = C // 2 * ["up0a", "qkv", "up1a", "end"].index(name) + j
                    v.tensor_tensor(branch[:, two, :], branch[:, two, :], wide(rp), ALU.mult).then_inc(prep_scaled, 1)
                    dve.wait_ge(prep_scaled, k + 1)
                    for c in (2 * j, 2 * j + 1):
                        last = v.scalar_tensor_tensor(out=x[:, c, :], in0=branch[:, c, :], scalar=vec(post, c),
                                                      in1=x[:, c, :], op0=ALU.mult, op1=ALU.add)
                    last.then_inc(prep_front, 1)
                elif name == "pw2":
                    v.tensor_tensor(branch[:, two, :], branch[:, two, :], wide(tA[:, 0, :]), ALU.subtract).then_inc(ln_step, 1)
                    dve.wait_ge(ln_step, LN_VAR + j + 1)
                    v.tensor_tensor(branch[:, two, :], branch[:, two, :], wide(rp), ALU.mult).then_inc(prep_front, 1)
                elif name == "out":
                    v.tensor_tensor(hn[:, two, :], hn[:, two, :], branch[:, two, :], ALU.mult).then_inc(prep_front, 1)

            def prep_back_part(name, j):
                k = C // 2 * prep_no[name] + j
                dve.wait_ge(prep_hi, k + 1)
                two = slice(2 * j, 2 * j + 2)
                if name in ("pw2", "out"):
                    src = branch if name == "pw2" else hn
                    v.tensor_tensor(xl[:, two, :], src[:, two, :], xh[:, two, :].bitcast(F32), ALU.subtract).then_inc(prep_lo, 1)
                else:
                    pre = {"pw1": "mix_pre0", "up0a": "ffn_pre0", "qkv": "mix_pre1", "up1a": "ffn_pre1"}[name]
                    for c in (2 * j, 2 * j + 1):
                        last = v.scalar_tensor_tensor(out=xl[:, c, :], in0=x[:, c, :], scalar=vec(pre, c),
                                                      in1=xh[:, c, :].bitcast(F32), op0=ALU.mult, op1=ALU.subtract)
                    last.then_inc(prep_lo, 1)

            def preps(name, first=(), then=()):
                n = C // 2
                out = {j: [lambda j=j: prep_back_part(name, j)] for j in range(n)}
                if name != "pw1":
                    for j in range(n):
                        out[max(0, j - 1)].insert(min(j, 1) if j < 2 else 0, lambda j=j: prep_front_part(name, j))
                out[0] = list(first) + out[0]
                out[n] = out.get(n, []) + list(then)
                return out

            for k in range(2):
                dve.wait_ge(vec_turned, k + 1)
                n = P + vec_rows[1] if k == 0 else n_wdw
                v.tensor_copy(vcol[:, (0 if k == 0 else 2 * P):(0 if k == 0 else 2 * P) + n], PS[:, k, 0:n]).then_inc(vec_ready, 1)
            dve.wait_ge(vec_ready, 2)
            first = ph["pw1"]
            for j in range(C // 2):
                prep_front_part("pw1", j)
            for n in range(AHEAD):
                split(first, 0, n, n)

            def zero_past():
                dve.wait_ge(x_turned, C)
                v.memset(u_prm[:, :, 0:TAIL], 0.0)

            window(first, 0, split, preps("pw1", then=[zero_past, lambda: inverse(1, rx)]))
            p = first
            dve.wait_ge(cache_ready, C // 2)
            with dve.Fori(1, p.groups - 1) as w:
                done[0] = w * p.units + (p.unit0 + AHEAD)
                window(p, w, split, conv_before(w - 1, w + (p.group0 - 1)))
            for w in range(p.groups - 1, p.groups):
                done[0] = w * p.units + (p.unit0 + AHEAD)
                window(p, w, split, conv_before(w - 1, w + (p.group0 - 1)))

            p = ph["pw2"]

            def last_conv():
                g = first.groups - 1
                glu_in_part(g, g)
                glu_out_part(g)
                conv_taps(g, g, range(W))

            def ln_stats():
                b = BANKS * ((p.group0 - 1) % 2)
                dve.wait_ge(stat_sum, 2)
                v.tensor_scalar(tA[:, 0, :], PS[:, b, 0:T], 1.0 / D, None, ALU.mult).then_inc(ln_step, 1)
                dve.wait_ge(ln_step, 1)
                v.tensor_tensor(tA[:, 1, :], tA[:, 0, :], tA[:, 0, :], ALU.mult).then_inc(ln_step, 1)
                dve.wait_ge(ln_step, 2)
                v.scalar_tensor_tensor(out=root[:, :], in0=PS[:, b + 1, 0:T], scalar=1.0 / D, in1=tA[:, 1, :],
                                       op0=ALU.mult, op1=ALU.subtract).then_inc(ln_step, 1)
                inverse(2, rp)

            window(p, 0, split, preps("pw2", first=[last_conv, ln_stats], then=[lambda: clear_acc()]))

            def squares_window(p, w):
                return {0: [lambda: add_squares(p, w - 1)]}

            def looped(p, make):
                with dve.Fori(1, p.groups - 1) as w:
                    done[0] = w * p.units + (p.unit0 + AHEAD)
                    window(p, w, split, make(w))
                w = p.groups - 1
                done[0] = w * p.units + (p.unit0 + AHEAD)
                window(p, w, split, make(w))

            looped(p, lambda w: squares_window(p, w))

            def ffn(l, k_inv, prev):
                a, da, b, db = (ph[f"{n}{l}{s_}"] for s_ in "ab" for n in ("up", "down"))
                window(a, 0, split, preps(f"up{l}a", first=[lambda: add_squares(prev, prev.groups - 1),
                                                           lambda: inverse(k_inv, rp)],
                                          then=[lambda: inverse(k_inv + 1, rx)]))
                for up, down in ((a, da), (b, db)):
                    e0 = up_first[up.name]

                    def up_window(w):
                        group, e = w + (up.group0 - 1), w + (e0 - 1)
                        return {0: [lambda: up_part1(up, w - 1)], 1: [lambda: up_part2(group, e)],
                                2: [lambda: up_part3(e, w * 2 - 2)]}

                    if up is b:
                        window(b, 0, split, {})
                    looped(up, up_window)
                    last = up_window(up.groups)
                    if down is db:
                        last[3] = [lambda: clear_acc()]
                    window(down, 0, split, last)
                    for w in range(1, down.groups):
                        window(down, w, split, {} if down is da else {0: [lambda: add_branch(db, w - 1, db.group0 + w - 1)]})

            dve.wait_ge(u_out, 16 * (B + 1))
            ffn(0, 3, ph["pw2"])

            p = ph["qkv"]

            def steps():
                k = [0]

                def link(ins):
                    k[0] += 1
                    ins.then_inc(row_dve, 1)
                    dve.wait_ge(row_dve, k[0])

                f32 = slice(32, 32 + H)
                dve.wait_ge(gate_mm, 1)
                dve.wait_ge(masks_ready, 5)
                v.scalar_tensor_tensor(out=i_row[:, :], in0=PS[0:H, 6, 0:T], scalar=1.0, in1=rx[0:H, :], op0=ALU.mult, op1=ALU.mult)
                link(v.tensor_tensor(f_row[:, :], PS[f32, 6, 0:T], rx[f32, :], ALU.mult))
                v.tensor_scalar(i_row[:, :], i_row[:, :], b_gate[:, 0:1], None, ALU.add)
                link(v.tensor_scalar(f_row[:, :], f_row[:, :], b_gate[:, 1:2], None, ALU.add))
                link(v.tensor_scalar(f_min[:, :], f_row[:, :], 0.0, None, ALU.min))
                link(v.scalar_tensor_tensor(out=f_abs[:, :], in0=f_row[:, :], scalar=-1.0, in1=f_row[:, :], op0=ALU.mult, op1=ALU.max))
                dve.wait_ge(row_act, 2)
                link(v.tensor_tensor(f_row[:, :], f_min[:, :], f_abs[:, :], ALU.subtract))
                link(v.tensor_tensor_scan(b_row[:, :], keep_row[:, :], f_row[:, :], 0.0, ALU.mult, ALU.add))
                link(v.tensor_tensor(c_row[:, :], i_row[:, :], b_row[:, :], ALU.subtract))
                link(v.tensor_tensor_scan(cum_row[:, :], cut_row[:, :], c_row[:, :], 0.0, ALU.add, ALU.max))
                v.tensor_scalar(rows[:, 0:TP], cum_row[:, 0:TP], 0.0, None, ALU.max)
                m0_wide = m0[:, :].rearrange("h (b t) -> h b t", t=1).broadcast_to([H, B, L])
                by_seq = lambda ap: ap.rearrange("h (b t) -> h b t", b=B)
                link(v.tensor_tensor(by_seq(rows[:, TP:T]), by_seq(cum_row[:, TP:T]), m0_wide, ALU.max))
                link(v.tensor_tensor(m_row[:, :], b_row[:, :], rows[:, 0:T], ALU.add))
                assert k[0] == M_STEPS, k[0]
                link(v.tensor_tensor(by_seq(rows[:, T:T + TS]), m0_wide, by_seq(rows[:, TP:T]), ALU.subtract))
                link(v.tensor_scalar(gr_row[:, 0:TP], c_row[:, 0:TP], rows[:, TP - 1:TP], None, ALU.subtract))
                m_last = rows[:, TP + L - 1:T:L].rearrange("h (b t) -> h b t", t=1).broadcast_to([H, B, L])
                link(v.tensor_tensor(by_seq(gr_row[:, TP:T]), by_seq(c_row[:, TP:T]), m_last, ALU.subtract))
                dve.wait_ge(row_turned, 1)
                cols = lambda r, k: PS[0:r, 5, k:k + 3 * H].rearrange("p (t h) -> p t h", t=3)
                for k0, dst in ((0, c_tok), (3 * H, gr_tok)):
                    v.tensor_copy(dst[:, 0:2, :], cols(P, k0)[:, 0:2, :])
                    v.tensor_copy(dst[0:TS, 2, :], cols(TS, k0)[:, 2, :])
                v.tensor_copy(n0T[:, :], PS[:, 5, 6 * H:6 * H + B * H]).then_inc(row_cols, 1)
                dve.wait_ge(row_cols, 1)
                dve.wait_ge(m_out, 32)

            def w_if_scale():
                dve.wait_ge(gates_in, 16 * 6)
                g_pre = vcol[:, v_at["mix_pre1"]:v_at["mix_pre1"] + C].rearrange("p (c n) -> p c n", n=1).broadcast_to([P, C, 40])
                v.tensor_tensor(w_if[:, :, :], w_if[:, :, :], g_pre, ALU.mult).then_inc(w_if_ready, 1)

            def qkv_out(h, group):
                fence()
                wait_bank(dve, ph["qkv"], h, 0)
                v.scalar_tensor_tensor(out=qT[:, :], in0=PS[:, 0, 0:T], scalar=float(DK) ** -0.5, in1=rx[:, :],
                                       op0=ALU.mult, op1=ALU.mult)
                v.tensor_scalar(rows_h[:, :], rows[:, :], ident[0:H, bass.ds(h, 1)], None, ALU.mult).then_inc(head_rows, 1)
                wait_bank(dve, ph["qkv"], h, 1)
                v.tensor_tensor(kT[:, :], PS[:, 1, 0:T], rx[:, :], ALU.mult)
                wait_bank(dve, ph["qkv"], h, 3)
                v.tensor_tensor(vT[:, :, :], PS[:, 2:4, 0:T], wide(rx), ALU.mult).then_inc(banks_read, 1)

            def cell_top(h):
                dve.wait_ge(tables, h + 1)
                col = lambda t, n, r=P: t[0:r, n, bass.ds(h, 1)]
                v.scalar_tensor_tensor(out=prob[:, 0:TP], in0=mask_p[:, :], scalar=col(c_tok, 0), in1=PS[:, 6, 0:TP],
                                       op0=ALU.add, op1=ALU.subtract)
                v.scalar_tensor_tensor(out=prob[:, TP:TP + P], in0=mask_p[:, 0:P], scalar=col(c_tok, 1), in1=PS[:, 6, P:TP],
                                       op0=ALU.add, op1=ALU.subtract)
                v.scalar_tensor_tensor(out=prob_s[:, :], in0=mask_s[:, :], scalar=col(c_tok, 2, TS), in1=PS[0:TS, 6, TP:T],
                                       op0=ALU.add, op1=ALU.subtract).then_inc(decay_in, 1)
                v.tensor_copy(g_state[:, :], PS[:, 6, T + L - 1:T + TS:L])
                v.tensor_tensor(qw[:, :], qT[:, TP:T], PS[:, 6, T:T + TS], ALU.mult).then_inc(qw_ready, 1)
                dve.wait_ge(qw_ready, h + 1)
                by_seq = lambda ap: ap.rearrange("p (b t) -> p b t", b=B)
                n_head = n0T[:, :].rearrange("p (b h) -> p h b", b=B)[:, bass.ds(h, 1), :].rearrange("p h b -> p (h b)")
                v.tensor_tensor(by_seq(qn[:, :]), by_seq(qw[:, :]),
                                n_head.rearrange("p (b t) -> p b t", t=1).broadcast_to([P, B, L]), ALU.mult).then_inc(qn_ready, 1)
                dve.wait_ge(kv_turned, h + 1)
                v.tensor_scalar(kw[0:TS, 2, :], PS[0:TS, 6, T + TS:T + TS + P], col(gr_tok, 2, TS), None, ALU.mult).then_inc(kw_ready, 1)
                for t in range(2):
                    v.tensor_scalar(kw[:, t, :], PS[:, 4, t * P:(t + 1) * P], col(gr_tok, t), None, ALU.mult)
                v.tensor_copy(v_tok[0:TS, 2, :], PS[0:TS, 4, 2 * P:4 * P]).then_inc(kw_ready, 1)
                dve.wait_ge(kw_ready, h * 2 + 2)
                v.tensor_tensor(kw_seq[:, :, :], kw[0:TS, 2, :].rearrange("s (a k) -> s a k", a=1).broadcast_to([TS, B, DK]),
                                seg[:, :].rearrange("s (b a) -> s b a", a=1).broadcast_to([TS, B, DK]), ALU.mult).then_inc(kw_seq_ready, 1)
                dve.wait_ge(decay_exp, h + 1)
                dve.wait_ge(scores, h + 1)
                v.tensor_tensor(prob[:, :], prob[:, :], PS[:, 7, 0:3 * P], ALU.mult)
                v.tensor_tensor(prob_s[:, :], prob_s[:, :], PS[0:TS, 7, 3 * P:3 * P + TS], ALU.mult).then_inc(prob_ready, 1)

            def cell_den(h):
                dve.wait_ge(den_abs, h + 1)
                v.tensor_tensor(tC[:, 0, :], root[:, :], PS[:, 7, 0:T], ALU.max).then_inc(den_max, 1)
                dve.wait_ge(den_max, h + 1)
                v.reciprocal(tC[:, 1, :], tC[:, 0, :]).then_inc(den_inv, 1)
                dve.wait_ge(den_inv, h + 1)
                dve.wait_ge(num_done, h + 1)
                v.tensor_tensor(hq[:, :, :], PS[:, 4:6, 0:T], wide(tC[:, 1, :]), ALU.mult).then_inc(hq_ready, 1)

            def cell_norm(h):
                dve.wait_ge(hq_rs, h + 1)
                for i in range(2):
                    last = v.scalar_tensor_tensor(out=hn[:, h * 2 + i, :], in0=hq[:, i, :],
                                                  scalar=vec("g_mh", h * 2 + i), in1=root[:, :], op0=ALU.mult, op1=ALU.mult)
                last.then_inc(hn_ready, 1)
                n_head = lambda t: t[:, 0:B * H].rearrange("p (b h) -> p h b", b=B)[:, bass.ds(h, 1), :].rearrange("p h b -> p (h b)")
                v.tensor_tensor(tC[:, 0, 0:B], n_head(n0T), g_state[:, :], ALU.mult).then_inc(n_scaled, 1)
                dve.wait_ge(n_scaled, h + 1)
                dve.wait_ge(Cp_read, h + 1)
                v.tensor_tensor(n_head(n_new), tC[:, 0, 0:B], Cn_prm[:, DV:DV + B], ALU.add)
                v.tensor_copy(n_new[:, bass.ds(h + B * H, 1)], Cn_prm[:, DV + B:DV + B + 1]).then_inc(n_done, 1)

            def cell_state(h, pair):
                dve.wait_ge(Cs_done, h * (B // 2) + (pair + 1))
                for i in range(2):
                    b = 2 * pair + i
                    v.scalar_tensor_tensor(out=C0[:, b, :], in0=C0[:, b, :], scalar=g_state[:, b:b + 1],
                                           in1=PS[:, 5 + 2 * (pair % 2), i * DV:(i + 1) * DV], op0=ALU.mult, op1=ALU.add).then_inc(C_new, 1)

            def cell_before(h, group):
                return {0: [lambda: qkv_out(h, group)], 1: [lambda: cell_top(h)], 3: [lambda: cell_den(h)],
                        4: [lambda: cell_norm(h)], 5: [lambda: cell_state(h, 0), lambda: cell_state(h, 1)],
                        6: [lambda: cell_state(h, 2)], 7: [lambda: cell_state(h, 3)]}

            before = preps("qkv", first=[lambda: add_branch(ph["down0b"], ph["down0b"].groups - 1, p.group0 - 1),
                                         lambda: inverse(5, rp)], then=[lambda: inverse(6, rx), steps])
            before[6].append(w_if_scale)
            window(p, 0, split, before)
            with dve.Fori(1, p.groups) as w:
                done[0] = w * p.units + (p.unit0 + AHEAD)
                window(p, w, split, cell_before(w - 1, w + (p.group0 - 1)))
            p = ph["o"]
            done[0] = p.unit0 + AHEAD
            window(p, 0, split, cell_before(H - 1, p.group0 - 1))

            def o_out(local, group):
                four = slice(local * BANKS, (local + 1) * BANKS)
                wait_bank(dve, ph["o"], local, 3)
                v.tensor_tensor(branch[:, four, :], PS[:, 0:BANKS, 0:T], wide(rx, BANKS), ALU.mult).then_inc(banks_read, 1)

            def o_finish(local):
                four = slice(local * BANKS, (local + 1) * BANKS)
                dve.wait_ge(o_exp, local + 1)
                v.tensor_scalar(branch[:, four, :], branch[:, four, :], 1.0, None, ALU.add).then_inc(o_plus, 1)
                dve.wait_ge(o_plus, local + 1)
                v.reciprocal(branch[:, four, :], branch[:, four, :]).then_inc(o_gate, 1)

            for w in range(1, p.groups):
                if w == 2:
                    dve.wait_ge(n_turned, 1)
                    v.tensor_copy(vrows[0:B * H + H, 0, :], PS[0:B * H + H, 7, 0:P]).then_inc(n_copied, 1)
                window(p, w, split, {0: [lambda: o_out(w - 1, p.group0 + w - 1)], 2: [lambda: o_finish(w - 1)]})
            p = ph["out"]

            def gates_ready():
                dve.wait_ge(o_gate, C // 4)

            window(p, 0, split, preps("out", first=[lambda: o_out(C // 4 - 1, p.group0 - 1), lambda: o_finish(C // 4 - 1), gates_ready],
                                      then=[lambda: clear_acc()]))
            looped(p, lambda w: squares_window(p, w))
            dve.wait_ge(C_out, 16 * H)
            dve.wait_ge(Cp_out, 16 * H)
            ffn(1, 7, ph["out"])

            db = ph["down1b"]
            add_branch(db, db.groups - 1, db.group0 + db.groups - 1)
            inverse(9, rp)
            for j in range(C // 2):
                prep_front_part("end", j)

        @block.tensor
        def _(pe):
            mm, turn = nc.tensor.matmul, nc.tensor.transpose

            def unit(p, g_bank, j, slot, n, rhs_hi, rhs_lo):
                pe.wait_ge(lo_done, n + 1)
                last_unit = j == p.units - 1
                for m in range(BANKS):
                    out = PS[:, g_bank + m, 0:T]
                    cols = slice(m * P, (m + 1) * P)
                    for kk in range(2):
                        k = 2 * j + kk
                        begin, end = k == 0, last_unit and kk == 1
                        mm(out, hi[:, slot, kk, cols], rhs_hi[:, k, :], start=begin, stop=False, skip_group_check=True)
                        mm(out, hi[:, slot, kk, cols], rhs_lo[:, k, :], start=False, stop=False, skip_group_check=True)
                        ins = mm(out, lo[:, slot, kk, cols], rhs_hi[:, k, :], start=False, stop=end, skip_group_check=True)
                    if last_unit and m < BANKS - 1:
                        ins.then_inc(bank_done, 1)
                ins.then_inc(units_used, 1)

            def group(p, g, before=None, single=False, rep=0):
                before = before or {}
                glob = g + p.group0
                rhs = (hh, hl) if p.name[:4] == "down" else (xh, xl)
                b = 0 if single else bank_of(glob)
                if not isinstance(g, int) or glob >= 2:
                    pe.wait_ge(banks_read, glob if single else glob - 1)
                for j in range(p.units):
                    for f in before.get(j, []):
                        f()
                    u = rep * p.units + j
                    n = g * p.units + (p.unit0 + j)
                    unit(p, b, j, u % SLOTS, n, *rhs)
                for f in before.get(p.units, []):
                    f()

            def phase(p, first=None, single=False):
                start = 0
                if first is not None:
                    group(p, 0, first, single)
                    start = 1
                with pe.Fori(start, p.groups) as g:
                    group(p, g, None, single)

            def sum_over_features(out, src, **kw_):
                return mm(out, ones[:, :], src, skip_group_check=True, **kw_)

            def wait_preps(name, j):
                pe.wait_ge(prep_lo, C // 2 * prep_no[name] + j + 1)

            def stat_rx(name, g):
                b = BANKS * (g % 2)
                cut = 512 - T
                pe.wait_ge(prep_sum, C * (sq_preps.index(name) + 1))
                sum_over_features(PS[:, b, T:512], accA[:, 0:cut], start=True, stop=True)
                sum_over_features(PS[:, b + 1, T:2 * T - cut], accA[:, cut:T], start=True, stop=True).then_inc(stat_sum, 1)

            def stat_post(no, g):
                pe.wait_ge(br_acc, (no + 1) * (C + 1))
                sum_over_features(PS[:, BANKS * ((g - 1) % 2), 0:T], acc[:, :], start=True, stop=True).then_inc(stat_sum, 1)

            def prep_windows(name, then=()):
                out = {j: [lambda j=j: wait_preps(name, j)] for j in range(C // 2)}
                out[C // 2] = list(then)
                return out

            pe.wait_ge(consts_ready, 5)
            pe.wait_ge(vec_in, 16 * (len(vec_dmas) + 4))
            for k in range(2):
                ins = turn(PS[:, 0, k * P:k * P + vec_rows[k]], vrows[0:vec_rows[k], k, :], ident[0:vec_rows[k], 0:vec_rows[k]])
            ins.then_inc(vec_turned, 1)
            for k in range(4):
                n = min(P, n_wdw - k * P)
                ins = turn(PS[:, 1, k * P:k * P + n], wdw_rows[0:n, k, :], ident[0:n, 0:n])
            ins.then_inc(vec_turned, 1)
            pe.wait_ge(x_in, 16 * 3)
            for c in range(C):
                if c >= 4:
                    pe.wait_ge(prep_front, (c - 4) // 2 + 1)
                cols = slice(c * P, (c + 1) * P)
                for t in range(2):
                    turn(PS[:, 4 + c % 4, t * P:(t + 1) * P], x_rows[:, t, cols], ident[:, :])
                turn(PS[:, 4 + c % 4, TP:T], x_rows2[:, cols], ident[0:TS, 0:TS]).then_inc(x_turned, 1)

            def cache_turn(j):
                if j == 0:
                    pe.wait_ge(cache_in, 16)
                    pe.wait_ge(prep_front, C // 2)
                if j >= 4:
                    pe.wait_ge(cache_ready, j - 3)
                half = B // 2 * TAIL
                for i in range(2):
                    c = 2 * j + i
                    for r in range(2):
                        ins = turn(PS[:, 4 + j % 4, (2 * i + r) * half:(2 * i + r + 1) * half], cache_rows[:, r, c * P:(c + 1) * P],
                                   ident[0:half, 0:half])
                ins.then_inc(cache_turned, 1)

            p = ph["pw1"]
            before = prep_windows("pw1", [lambda: stat_rx("pw1", 0)])
            for j in range(C // 2):
                before[j].append(lambda j=j: cache_turn(j))
            group(p, 0, before)
            pe.wait_ge(cache_ready, C // 2)
            with pe.Fori(1, p.groups) as g:
                group(p, g)

            p = ph["pw2"]
            pe.wait_ge(banks_read, p.group0)
            pe.wait_ge(u_packed, 1)
            for half in range(2):
                for k in range(C // 4):
                    bank = (k + BANKS * (1 - half) + BANKS * (p.group0 % 2)) % 8
                    for i in range(4):
                        c = 4 * k + i
                        if half == 0:
                            ins = turn(PS[0:TS, bank, i * P:(i + 1) * P], u_new[:, c, :], ident[:, :])
                        else:
                            ins = turn(PS[0:TAIL, bank, i * P:(i + 1) * P], u_prm[:, c, TP:TP + TAIL], ident[:, :])
                    ins.then_inc(u_turned, 1)
            pe.wait_ge(conv_sum, 2 * C + 2)
            pe.wait_ge(u_copied, C // 2)
            b = BANKS * ((p.group0 - 1) % 2)
            sum_over_features(PS[:, b, 0:T], accA[:, :], start=True, stop=True)
            sum_over_features(PS[:, b + 1, 0:T], accB[:, :], start=True, stop=True).then_inc(stat_sum, 1)
            phase(p, prep_windows("pw2"))

            def ffn(l, no):
                a, da, b_, db = (ph[f"{n}{l}{s_}"] for s_ in "ab" for n in ("up", "down"))
                stat_post(no, a.group0)
                phase(a, prep_windows(f"up{l}a", [lambda: stat_rx(f"up{l}a", a.group0)]))

                def wait_h(up, j):
                    pe.wait_ge(h_ready, up_first[up.name] + j + 1)

                group(da, 0, {j: [lambda j=j: wait_h(a, j)] for j in range(da.units)})
                with pe.Fori(1, da.groups) as g:
                    group(da, g)
                phase(b_)
                with pe.Fori(0, db.groups // 2) as it:
                    group(db, it * 2, {j: [lambda j=j: wait_h(b_, j)] for j in range(db.units)}, rep=0)
                    group(db, it * 2 + 1, rep=1)

            ffn(0, 0)

            p = ph["qkv"]
            stat_post(1, p.group0)

            def gates():
                pe.wait_ge(w_if_ready, 2)
                for c in range(C):
                    ins = mm(PS[0:40, 6, 0:T], w_if[:, c, :], x[:, c, :], start=(c == 0), stop=(c == C - 1), skip_group_check=True)
                ins.then_inc(gate_mm, 1)

            def turn_rows():
                pe.wait_ge(row_act, 3)
                for k0, src in ((0, c_row), (3 * H, gr_row)):
                    for t in range(3):
                        n = P if t < 2 else TS
                        turn(PS[0:n, 5, k0 + t * H:k0 + (t + 1) * H], src[:, t * P:t * P + n], ident[0:H, 0:H])
                turn(PS[:, 5, 6 * H:6 * H + B * H], n0_rows[:, :], ident[0:B * H, 0:B * H]).then_inc(row_turned, 1)

            def cell_top(h):
                pe.wait_ge(head_rows, h + 1)
                pe.wait_ge(C_new, h * B)
                pe.wait_ge(Cp_read, h)
                mm(PS[:, 6, 0:T + TS], ones[0:H, :], rows_h[:, 0:T + TS], start=True, stop=True, skip_group_check=True).then_inc(tables, 1)
                pe.wait_ge(banks_read, h + (ph["qkv"].group0 + 1))
                mm(PS[:, 7, 0:TP], kT[:, 0:P], qT[:, 0:TP], start=True, stop=True, skip_group_check=True)
                mm(PS[:, 7, TP:TP + P], kT[:, P:TP], qT[:, P:TP], start=False, stop=True, skip_group_check=True)
                mm(PS[0:TS, 7, 3 * P:3 * P + TS], kT[:, TP:T], qT[:, TP:T], start=False, stop=True, skip_group_check=True).then_inc(scores, 1)
                for t in range(2):
                    turn(PS[:, 4, t * P:(t + 1) * P], kT[:, t * P:(t + 1) * P], ident[:, :])
                    for i in range(2):
                        if t and i:
                            pe.wait_ge(qw_ready, h + 1)
                        turn(PS[:, 5, (2 * t + i) * P:(2 * t + i + 1) * P], vT[:, i, t * P:(t + 1) * P], ident[:, :])
                for i in range(2):
                    turn(PS[0:TS, 4, (2 + i) * P:(3 + i) * P], vT[:, i, TP:T], ident[:, :])
                turn(PS[0:TS, 6, T + TS:T + TS + P], kT[:, TP:T], ident[:, :]).then_inc(kv_turned, 1)

            def cell_num(h):
                pe.wait_ge(prob_ready, h + 1)
                pe.wait_ge(kw_seq_ready, h + 1)
                pe.wait_ge(v_ready, h + 1)
                pe.wait_ge(qn_ready, h + 1)
                pe.wait_ge(C0_in, h * 16 + 16)

                def intra(bank, lhs):
                    mm(PS[:, bank, 0:TP], lhs(0, P), prob[:, 0:TP], start=True, stop=False, skip_group_check=True)
                    mm(PS[:, bank, P:TP], lhs(1, P), prob[:, TP:TP + P], start=False, stop=False, skip_group_check=True)
                    mm(PS[:, bank, TP:T], lhs(2, TS), prob_s[:, :], start=False, stop=False, skip_group_check=True)

                intra(6, lambda t, n: ones[0:n, :])
                mm(PS[:, 6, TP:T], ones[:, :], qn[:, :], start=False, stop=True, skip_group_check=True)
                mm(PS[:, 7, 0:T], ones[0:H, :], rows_h[:, T + TS:2 * T + TS], start=True, stop=True,
                   skip_group_check=True).then_inc(den_done, 1)
                for i in range(2):
                    cols = slice(i * P, (i + 1) * P)
                    intra(4 + i, lambda t, n: v_tok[0:n, t, cols])
                    for b in range(B):
                        ins = mm(PS[:, 4 + i, TP + b * L:TP + (b + 1) * L], C0[:, b, cols], qw[:, b * L:(b + 1) * L],
                                 start=False, stop=True, skip_group_check=True)
                ins.then_inc(num_done, 1)

            def state_pair(h, pair):
                for i in range(2):
                    ins = mm(PS[:, 5 + 2 * (pair % 2), i * DV:(i + 1) * DV], kw_seq[:, 2 * pair + i, :], v_tok[0:TS, 2, :],
                             start=(i == 0), stop=True, skip_group_check=True)
                ins.then_inc(Cs_done, 1)

            def cell_norm(h):
                pe.wait_ge(hq_sq, h + 1)
                mm(PS[:, 6, 0:T], ones[:, :], sq[:, 0, 0, :], start=True, stop=False, skip_group_check=True)
                mm(PS[:, 6, 0:T], ones[:, :], sq[:, 0, 1, :], start=False, stop=True, skip_group_check=True).then_inc(hq_sum, 1)
                mm(PS[:, 4, 0:DV], kw[:, 0, :], v_tok[:, 0, :], start=True, stop=False, skip_group_check=True)
                mm(PS[:, 4, 0:DV], kw[:, 1, :], v_tok[:, 1, :], start=False, stop=True, skip_group_check=True)
                mm(PS[:, 4, DV:DV + B], kw[0:TS, 2, :], seg[:, :], start=False, stop=True, skip_group_check=True)
                mm(PS[:, 4, DV + B:DV + B + 1], kw[:, 0, :], ones[:, 0:1], start=False, stop=False, skip_group_check=True)
                mm(PS[:, 4, DV + B:DV + B + 1], kw[:, 1, :], ones[:, 0:1], start=False, stop=True, skip_group_check=True).then_inc(Cp_done, 1)
                state_pair(h, 0)
                state_pair(h, 1)

            def cell_state(h):
                pe.wait_ge(C_new, h * B + 2)
                state_pair(h, 2)
                pe.wait_ge(C_new, h * B + 4)
                state_pair(h, 3)

            def cell_before(h):
                return {1: [lambda: cell_top(h)], 4: [lambda: cell_num(h)], 6: [lambda: cell_norm(h)], 7: [lambda: cell_state(h)]}

            before = prep_windows("qkv", [lambda: stat_rx("qkv", p.group0), gates, turn_rows])
            group(p, 0, before, single=True)
            pe.wait_ge(row_cols, 1)
            with pe.Fori(1, p.groups) as g:
                group(p, g, cell_before(g - 1), single=True)
            o = ph["o"]
            group(o, 0, cell_before(H - 1), single=True)
            pe.wait_ge(n_done, H)
            pe.wait_ge(C_new, H * B)
            turn(PS[0:B * H + H, 7, 0:P], n_new[:, :], ident[:, :]).then_inc(n_turned, 1)
            with pe.Fori(1, o.groups) as g:
                group(o, g, None, single=True)
            p = ph["out"]
            pe.wait_ge(banks_read, p.group0 + 0)
            phase(p, prep_windows("out"))
            ffn(1, 2)

            end = ph["down1b"].group0 + ph["down1b"].groups
            stat_post(3, end)
            for k in range(C // 4):
                pe.wait_ge(prep_front, C // 2 * prep_no["end"] + 2 * k + 2)
                for t in range(3):
                    i = 3 * k + t
                    n = P if t < 2 else TS
                    if i >= 8:
                        pe.wait_ge(y_copied, i - 7)
                    for c in range(4):
                        ins = turn(PS[0:n, i % 8, c * P:(c + 1) * P], x[:, 4 * k + c, t * P:t * P + n], ident[:, :])
                    ins.then_inc(y_turned, 1)


_INS = ["x_prompt", "x_sample", "cache_conv", "state_C", "state_n", "state_m", "conv_w_pw1", "conv_b_pw1",
        "conv_w_dw", "conv_b_dw", "conv_ln_g", "conv_ln_b", "conv_w_pw2", "conv_b_pw2", "mlstm_w_q", "mlstm_w_k",
        "mlstm_w_v", "mlstm_w_o", "mlstm_w_i", "mlstm_b_i", "mlstm_w_f", "mlstm_b_f", "mlstm_g_norm",
        "mlstm_w_out", "ffn_w_gate", "ffn_w_up", "ffn_w_down", "norm_mix_pre", "norm_mix_post", "norm_ffn_pre",
        "norm_ffn_post"]


def kernel(**inputs):
    import numpy as np
    import concourse.bacc as bacc
    from concourse.bass_utils import run_bass_kernel_spmd

    b, tp, d = inputs["x_prompt"].shape
    bs, ts, _ = inputs["x_sample"].shape
    nl, _, tail, _ = inputs["cache_conv"].shape
    nm, _, heads, dk, dv = inputs["state_C"].shape
    outs = [("y_prompt", (b, tp, d)), ("y_sample", (bs, ts, d)), ("conv_prompt", (nl, b, tail, d)),
            ("conv_sample", (nl, bs, tail, d)), ("C_prompt", (nm, b, heads, dk, dv)), ("n_prompt", (nm, b, heads, dk)),
            ("m_prompt", (nm, b, heads)), ("C_sample", (nm, bs, heads, dk, dv)), ("n_sample", (nm, bs, heads, dk)),
            ("m_sample", (nm, bs, heads))]
    nc = bacc.Bacc("TRN2", target_bir_lowering=False, num_devices=1, dynamic_dma_scratch_size=4096)
    arrays, args = {}, []
    for name in _INS:
        a = np.ascontiguousarray(inputs[name])
        arrays[f"in_{name}"] = a
        args.append(nc.dram_tensor(f"in_{name}", a.shape, mybir.dt.from_np(a.dtype), kind="ExternalInput").ap())
    for name, shape in outs:
        args.append(nc.dram_tensor(f"out_{name}", shape, F32, kind="ExternalOutput").ap())
    trunk_kernel(nc, *args)
    r = run_bass_kernel_spmd(nc, [arrays], core_ids=[0])
    return tuple(r.results[0][f"out_{name}"] for name, _ in outs)
```

```python
from contextlib import ExitStack

import concourse.bass as bass
from concourse import mybir

ALU = mybir.AluOpType
ACT = mybir.ActivationFunctionType
F32 = mybir.dt.float32
F32R = mybir.dt.float32r

P = 128
BIG = -1.0e30
AHEAD = 3
SLOTS = 4
BANKS = 4


class Phase:

    def __init__(self, name, units, groups, dmas):
        self.name, self.units, self.groups, self.dmas = name, units, groups, dmas


def plan(C, FC, H):
    segs = [24, FC - 24]
    ups = lambda l: [Phase(f"up{l}a", C // 2, segs[0] // 2, 2), Phase(f"down{l}a", segs[0] // 2, C // 4, 2),
                     Phase(f"up{l}b", C // 2, segs[1] // 2, 2), Phase(f"down{l}b", segs[1] // 2, C // 4, 2)]
    order = [Phase("pw1", C // 2, C // 2, 2), Phase("pw2", C // 2, C // 4, 2), *ups(0),
             Phase("qkv", C // 2, H, 3), Phase("o", C // 2, C // 4, 3), Phase("out", C // 2, C // 4, 2), *ups(1)]
    unit = group = landed = 0
    for p in order:
        p.unit0, p.group0, p.landed0 = unit, group, landed
        unit += p.units * p.groups
        group += p.groups
        landed += p.units * p.groups // SLOTS * 16 * p.dmas
    return order, unit, segs


def trunk_kernel(
    nc: bass.Bass,
    x_prompt: bass.AP, x_sample: bass.AP, cache_conv: bass.AP, state_C: bass.AP, state_n: bass.AP,
    state_m: bass.AP, conv_w_pw1: bass.AP, conv_b_pw1: bass.AP, conv_w_dw: bass.AP,
    conv_b_dw: bass.AP, conv_ln_g: bass.AP, conv_ln_b: bass.AP, conv_w_pw2: bass.AP,
    conv_b_pw2: bass.AP, mlstm_w_q: bass.AP, mlstm_w_k: bass.AP, mlstm_w_v: bass.AP,
    mlstm_w_o: bass.AP, mlstm_w_i: bass.AP, mlstm_b_i: bass.AP, mlstm_w_f: bass.AP,
    mlstm_b_f: bass.AP, mlstm_g_norm: bass.AP, mlstm_w_out: bass.AP, ffn_w_gate: bass.AP,
    ffn_w_up: bass.AP, ffn_w_down: bass.AP, norm_mix_pre: bass.AP, norm_mix_post: bass.AP,
    norm_ffn_pre: bass.AP, norm_ffn_post: bass.AP,
    y_prompt: bass.AP, y_sample: bass.AP, conv_prompt: bass.AP, conv_sample: bass.AP,
    C_prompt: bass.AP, n_prompt: bass.AP, m_prompt: bass.AP,
    C_sample: bass.AP, n_sample: bass.AP, m_sample: bass.AP,
):
    _, TP, D = x_prompt.shape
    B, L, _ = x_sample.shape
    TS = B * L
    T = TP + TS
    C = D // P
    _, _, H, DK, DV = state_C.shape
    W = conv_w_dw.shape[1]
    TAIL = W - 1
    DFF = ffn_w_gate.shape[2]
    FC = DFF // P
    assert DK == P and DV == 2 * P and TP == 2 * P and TS <= 64 and C == 2 * H
    RMS_EPS, LN_EPS = 1e-6, 1e-5
    phases, n_units, segs = plan(C, FC, H)
    ph = {p.name: p for p in phases}
    UNSPLIT = ph["pw1"].units * ph["pw1"].groups
    follows = {p.name: q for p, q in zip(phases, phases[1:])}
    PREPS = ["pw1", "pw2", "up0a", "qkv", "out", "up1a", "end"]
    prep_no = {name: i for i, name in enumerate(PREPS)}
    up_first = {"up0a": 0, "up0b": segs[0] // 2, "up1a": FC // 2, "up1b": FC // 2 + segs[0] // 2}
    seg_of = {"a": 0, "b": segs[0]}
    sq_no = {"pw2": 0, "down0b": 1, "out": 2, "down1b": 3}
    sq_preps = ["pw1", "up0a", "qkv", "up1a"]
    posts = ["up0a", "qkv", "up1a", "end"]
    POST_K = [3, 5, 7, 9]
    ROOTS = [0, 2, 3, 4, 6, 7, 9, 10, 12, 13]
    LN_VAR = 3
    M_STEPS = 10

    ctx = ExitStack()
    with ctx:
        def sem(name):
            return ctx.enter_context(nc.semaphore(name))

        at = [(nc.sbuf_base + 63) // 64 * 64]

        def sb(name, shape, dt=F32, place=None):
            size = 4
            for n in shape[1:]:
                size *= n
            where = at[0] if place is None else place[0]
            nxt = (where + size + 31) // 32 * 32
            if place is None:
                at[0] = nxt
            else:
                place[0] = nxt
            return nc.alloc_sbuf_tensor_at(name, list(shape), dt, offset=where)

        x = sb("x", [P, C, T])
        xh = sb("xh", [P, C, T], F32R)
        xl_at = at[0]
        xl = sb("xl", [P, C, T], F32R)
        xg = sb("xg", [P, C, T], place=[at[0] - 2 * C * T * 4])
        assert at[0] % 32 == 0 and (C * T * 4) % 32 == 0
        branch_at = [at[0]]
        branch = sb("branch", [P, C, T])
        raw = sb("raw", [P, SLOTS, 2, 512])
        hi = sb("hi", [P, SLOTS, 2, 512], F32R)
        lo = sb("lo", [P, SLOTS, 2, 512], F32R)
        shared_at = at[0]
        hh = sb("hh", [P, segs[0], T], F32R)
        hl = sb("hl", [P, segs[0], T], F32R)
        shared_end = at[0]
        vrows = sb("vrows", [P, 2, P])
        n_wdw = W * C
        vcol = sb("vcol", [P, 2 * P + n_wdw])
        ident = sb("ident", [P, P])
        ones = sb("ones", [P, P])
        eps = sb("eps", [P, 2])
        rx = sb("rx", [P, T])
        rp = sb("rp", [P, T])
        root = sb("root", [P, T])
        sq = sb("sq", [P, 2, 2, T])
        acc = sb("acc", [P, T])
        accA = sb("accA", [P, T])
        accB = sb("accB", [P, T])
        tA = sb("tA", [P, 2, T])
        tB_at = at[0]
        tB = sb("tB", [P, 2, T])
        w_if = sb("w_if", [P, C, 40])
        n0_rows = sb("n0_rows", [B * H, P])
        b_gate = sb("b_gate", [H, 2])
        m0 = sb("m0", [H, B])
        mask_p = sb("mask_p", [P, TP])
        mask_s = sb("mask_s", [TS, TS])
        seg = sb("seg", [TS, B])
        assert at[0] <= nc.sbuf_usable_end, at[0]

        here = [shared_at]
        u_smp = sb("u_smp", [P, C, B, TAIL + L], place=here)
        u_rows_at = here[0]
        cache_rows = sb("cache_rows", [B // 2 * TAIL, 2, D], place=here)
        u_rows = sb("u_rows", [TS, 2, D], place=[u_rows_at])
        u_prm_at = here[0]
        u_prm = sb("u_prm", [P, C, TAIL + TP], place=here)
        x_rows2 = sb("x_rows2", [TS, D], place=[u_prm_at])
        assert here[0] <= shared_end
        x_rows = sb("x_rows", [P, 2, D], place=[branch_at[0]])
        wdw_rows = sb("wdw_rows", [P, 4, P], place=here)
        u_new = sb("u_new", [P, C, TS], place=here)
        assert here[0] <= shared_end
        spare = [xl_at]
        pair = lambda name, *shape: sb(name, [P, *shape], place=spare)
        u_pair = pair("u_pair", 2, B, TAIL + L)
        w_pair = pair("w_pair", W, 2)
        b_pair = pair("b_pair", 2)
        prod = pair("prod", 2, 2, TS)
        y_pair = pair("y_pair", 2, TS)
        assert here[0] <= shared_end
        here = [shared_at]
        cell = lambda name, shape: sb(name, shape, place=here)
        hn = cell("hn", [P, C, T])
        qT = cell("qT", [P, T])
        kT = cell("kT", [P, T])
        vT = cell("vT", [P, 2, T])
        v_tok = cell("v_tok", [P, 3, DV])
        kw = cell("kw", [P, 3, DK])
        kw_seq = cell("kw_seq", [TS, B, DK])
        prob = cell("prob", [P, 3 * P])
        prob_s = cell("prob_s", [TS, TS])
        rows = cell("rows", [H, 2 * T + TS])
        rows_h = cell("rows_h", [H, 2 * T + TS])
        C0 = cell("C0", [P, B, DV])
        qw_seq = cell("qw_seq", [P, B, TS])
        inter = cell("inter", [TS, DV])
        qn = cell("qn", [P, TS])
        g_state = cell("g_state", [P, B])
        hq = cell("hq", [P, 2, T])
        Cn_prm = cell("Cn_prm", [P, DV + B + 1])
        c_tok = cell("c_tok", [P, 3, H])
        gr_tok = cell("gr_tok", [P, 3, H])
        tC = cell("tC", [P, 2, T])
        n0T = cell("n0T", [P, B * H])
        n_new = cell("n_new", [P, B * H + H])
        assert here[0] <= shared_end, (here[0], shared_end)
        here = [shared_at]
        row = lambda name, n=T: sb(name, [H, n], place=here)
        i_row, f_row, f_abs, f_min, b_row, c_row, keep_row, cut_row, gr_row, cum_row = (
            row(n) for n in ("i_row", "f_row", "f_abs", "f_min", "b_row", "c_row",
                             "keep_row", "cut_row", "gr_row", "cum_row"))
        m_row = sb("m_row", [H, T], place=[tB_at])
        assert here[0] <= shared_at + C * T * 4
        here = [shared_at]
        y_rows = sb("y_rows", [P, 3, D], place=here)
        PS = ctx.enter_context(nc.psum_tensor("PS", [P, 8, 512], F32))

        v_at = {}
        vec_dmas = []
        for k, (name, ap) in enumerate((("mix_pre", norm_mix_pre), ("mix_post", norm_mix_post),
                                        ("ffn_pre", norm_ffn_pre), ("ffn_post", norm_ffn_post))):
            for l in range(2):
                v_at[f"{name}{l}"] = 2 * C * k + C * l
            vec_dmas.append((2 * C * k, 2 * C, 0, ap.rearrange("l (c p) -> (l c) p", p=P)))
        r0 = 0
        for name, ap, n in (("b_pw1", conv_b_pw1, 2 * C), ("b_dw", conv_b_dw, C), ("ln_g", conv_ln_g, C),
                            ("ln_b", conv_ln_b, C), ("b_pw2", conv_b_pw2, C), ("g_mh", mlstm_g_norm, C)):
            v_at[name] = P + r0
            vec_dmas.append((r0, n, 1, ap.rearrange("l (c p) -> (l c) p", p=P)))
            r0 += n
        vec_rows = [P, r0]
        v_at["w_dw"] = 2 * P

        def vec(name, c, n=1):
            return vcol[:, bass.ds(c + v_at[name], n)]

        raw_in = [sem(f"raw_in{s}") for s in range(SLOTS)]
        hi_done, lo_done, units_used = sem("hi_done"), sem("lo_done"), sem("units_used")
        bank_done = sem("bank_done")
        banks_read = sem("banks_read")
        x_in = [sem("x_in0"), sem("x_in1")]
        vec_in, wdw_in, cache_in, gates_in, C0_in = (sem(n) for n in ("vec_in", "wdw_in", "cache_in", "gates_in", "C0_in"))
        consts_ready, vec_turned, vec_ready = sem("consts_ready"), sem("vec_turned"), sem("vec_ready")
        x_turned, cache_turned, cache_ready = sem("x_turned"), sem("cache_turned"), sem("cache_ready")
        prep_scaled, pair_scaled, prep_front, prep_act = sem("prep_scaled"), sem("pair_scaled"), sem("prep_front"), sem("prep_act")
        prep_sq, prep_hi, prep_lo, prep_sum = sem("prep_sq"), sem("prep_hi"), sem("prep_lo"), sem("prep_sum")
        stat_sum, stat_root, stat_inv, ln_step = sem("stat_sum"), sem("stat_root"), sem("stat_inv"), sem("ln_step")
        sums_clear = sem("sums_clear")
        br_out, br_sq, br_acc = sem("br_out"), sem("br_sq"), sem("br_acc")
        up_gate, up_silu, up_prod, up_hi, h_ready = (sem(n) for n in ("up_gate", "up_silu", "up_prod", "up_hi", "h_ready"))
        glu_in, glu_sig, conv_step, conv_sq, conv_sum, smp_step, smp_out = (
            sem(n) for n in ("glu_in", "glu_sig", "conv_step", "conv_sq", "conv_sum", "smp_step", "smp_out"))
        u_packed, u_turned, u_copied, u_out = sem("u_packed"), sem("u_turned"), sem("u_copied"), sem("u_out")
        gate_mm, row_dve, row_act, row_turned, row_cols = (
            sem(n) for n in ("gate_mm", "row_dve", "row_act", "row_turned", "row_cols"))
        masks_ready, w_if_ready = sem("masks_ready"), sem("w_if_ready")
        head_rows, tables, scores, kv_turned = sem("head_rows"), sem("tables"), sem("scores"), sem("kv_turned")
        decay_in, decay_exp, qw_ready, qn_ready = sem("decay_in"), sem("decay_exp"), sem("qw_ready"), sem("qn_ready")
        kw_ready, kw_seq_ready, v_ready, prob_ready = sem("kw_ready"), sem("kw_seq_ready"), sem("v_ready"), sem("prob_ready")
        den_done, den_abs, den_max, den_inv, num_done = (sem(n) for n in ("den_done", "den_abs", "den_max", "den_inv", "num_done"))
        inter_done, inter_ready = sem("inter_done"), sem("inter_ready")
        hq_ready, hq_sq, hq_sum, hq_ln, hq_rs = (
            sem(n) for n in ("hq_ready", "hq_sq", "hq_sum", "hq_ln", "hq_rs"))
        Cp_done, Cp_read, Cs_done, C_new, n_scaled, n_done = (
            sem(n) for n in ("Cp_done", "Cp_read", "Cs_done", "C_new", "n_scaled", "n_done"))
        o_gate = sem("o_gate")
        C_out, Cp_out, m_out, n_turned, n_copied, y_turned, y_copied, y_out, stored = (
            sem(n) for n in ("C_out", "Cp_out", "m_out", "n_turned", "n_copied", "y_turned", "y_copied", "y_out", "stored"))

        def landed(phase, k, s):
            return phase.landed0 + 16 * phase.dmas * (k + 1)

        def bank_of(group):
            return (group % 2) * BANKS

        def wait_bank(eng, p, g, m):
            if m < BANKS - 1:
                eng.wait_ge(bank_done, g * 3 + (3 * p.group0 + m + 1))
            else:
                eng.wait_ge(units_used, g * p.units + (p.unit0 + p.units))

        def acc_count(p, g, m):
            return g * BANKS + (sq_no[p.name] * (C + 1) + 1 + m)

        def out_count(p, g):
            return g * 3 + sq_no[p.name] * 3 * (C // BANKS)

        def weight_dmas(p, g, j, slot):
            pair = lambda ap: ap.rearrange("(k p) n -> p k n", p=P)
            rows2 = lambda w, first: pair(w)[:, first:first + 2, :]
            half = BANKS // 2 * P
            if p.name == "pw1":
                w = rows2(conv_w_pw1[0], 2 * j)
                yield raw[:, slot, :, 0:half], w[:, :, bass.ds(g * half, half)]
                yield raw[:, slot, :, half:2 * half], w[:, :, bass.ds(g * half + D, half)]
            elif p.name[:2] == "up":
                l, s0 = int(p.name[2]), seg_of[p.name[3]] * P
                yield raw[:, slot, :, 0:half], rows2(ffn_w_gate[l], 2 * j)[:, :, bass.ds(g * half + s0, half)]
                yield raw[:, slot, :, half:2 * half], rows2(ffn_w_up[l], 2 * j)[:, :, bass.ds(g * half + s0, half)]
            elif p.name == "qkv":
                yield raw[:, slot, :, 0:P], rows2(mlstm_w_q[0], 2 * j)[:, :, bass.ds(g * P, P)]
                yield raw[:, slot, :, P:2 * P], rows2(mlstm_w_k[0], 2 * j)[:, :, bass.ds(g * P, P)]
                yield raw[:, slot, :, 2 * P:4 * P], rows2(mlstm_w_v[0], 2 * j)[:, :, bass.ds(g * DV, DV)]
            else:
                w, first = {"pw2": (conv_w_pw2[0], 0), "o": (mlstm_w_o[0], 0), "out": (mlstm_w_out[0], 0)}.get(
                    p.name) or (ffn_w_down[int(p.name[4])], seg_of[p.name[5]])
                w = rows2(w, first + 2 * j)[:, :, bass.ds(g * 512, 512)]
                yield raw[:, slot, 0, :], w[:, 0, :]
                if p.dmas == 2:
                    yield raw[:, slot, 1, :], w[:, 1, :]
                else:
                    yield raw[:, slot, 1, 0:256], w[:, 1, 0:256]
                    yield raw[:, slot, 1, 256:512], w[:, 1, 256:512]

        block = ctx.enter_context(nc.Block())

        @block.sync
        def _(sp):
            for k in range(2):
                cols = slice(k * D // 2, (k + 1) * D // 2)
                for t in range(2):
                    sp.dma_start(x_rows[:, t, cols], x_prompt[0, t * P:(t + 1) * P, cols]).then_inc(x_in[k], 16)
                sp.dma_start(x_rows2[:, cols], x_sample.rearrange("b t d -> (b t) d")[:, cols]).then_inc(x_in[k], 16)
                if k == 0:
                    sp.wait_ge(vec_in, 16 * len(vec_dmas))

            def load(p, g, j, k_in_phase, n):
                slot = j % SLOTS if p.units % SLOTS == 0 else k_in_phase % SLOTS
                if p is ph["pw1"] or isinstance(n, int) and n < UNSPLIT + SLOTS:
                    if not isinstance(n, int) or n >= SLOTS:
                        sp.wait_ge(units_used, n - (SLOTS - 1))
                else:
                    sp.wait_ge(lo_done, n - (SLOTS - 1 + UNSPLIT))
                for dst, src in weight_dmas(p, g, j, slot):
                    sp.dma_start(dst, src).then_inc(raw_in[slot], 16)

            for p in phases:
                per = 1 if p.units % SLOTS == 0 else 2
                first = 0
                if p.name in ("pw1", "pw2"):
                    for j in range(p.units):
                        load(p, 0, j, j, p.unit0 + j)
                    first = 1
                with sp.Fori(first, p.groups // per) as it:
                    for r in range(per):
                        for j in range(p.units):
                            load(p, it * per + r, j, r * p.units + j, it * (per * p.units) + (p.unit0 + r * p.units + j))

            for k in range(C // 4):
                cols = slice(512 * k, 512 * (k + 1))
                sp.wait_ge(y_copied, 3 * (k + 1))
                for t in range(2):
                    sp.dma_start(y_prompt[0, t * P:(t + 1) * P, cols], y_rows[:, t, cols]).then_inc(y_out, 16)
                sp.dma_start(y_sample.rearrange("b t d -> (b t) d")[:, cols], y_rows[0:TS, 2, cols]).then_inc(y_out, 16)
            sp.wait_ge(y_out, 16 * 3 * (C // 4))

        @block.gpsimd
        def _(pool):
            g = nc.gpsimd
            g.memset(ident[:, :], 0.0).then_inc(consts_ready, 1)
            pool.wait_ge(consts_ready, 1)
            g.affine_select(out=ident[:, :], in_=ident[:, :], compare_op=ALU.not_equal, fill=1.0, base=0,
                            pattern=[[-1, P]], channel_multiplier=1).then_inc(consts_ready, 1)
            g.memset(ones[:, :], 1.0).then_inc(consts_ready, 1)
            g.memset(eps[:, 0:1], RMS_EPS).then_inc(consts_ready, 1)
            g.memset(eps[:, 1:2], LN_EPS).then_inc(consts_ready, 1)
            pool.dma_start(cache_rows[:, :, :], cache_conv[0].rearrange("(r b) t d -> (b t) r d", r=2)).then_inc(cache_in, 16)
            pool.dma_start(conv_sample[0, :, 0:TAIL - L, :], cache_conv[0, :, L:TAIL, :]).then_inc(stored, 16)

            def clear_sums(k, *sums):
                for s in sums:
                    last = g.memset(s[:, :], 0.0)
                last.then_inc(sums_clear, 1)
                pool.wait_ge(sums_clear, k)

            def scale_pair(name, j):
                two = slice(2 * j, 2 * j + 2)
                g.tensor_tensor(branch[:, two, :], branch[:, two, :],
                                rp[:, :].rearrange("p (a t) -> p a t", a=1).broadcast_to([P, 2, T]),
                                ALU.mult).then_inc(pair_scaled, 1)

            def sum_prep(name, k_clear):
                q0 = C // 2 * sq_preps.index(name)
                if k_clear > 2:
                    pool.wait_ge(prep_sum, 2 * q0)
                    pool.wait_ge(stat_root, ROOTS[2 * k_clear - 2])
                clear_sums(k_clear, accA)
                if name in posts:
                    pool.wait_ge(stat_inv, POST_K[posts.index(name)])
                    scale_pair(name, 1)
                for j in range(C // 2):
                    if name in posts and j + 2 < C // 2:
                        scale_pair(name, j + 2)
                    pool.wait_ge(prep_sq, q0 + j + 1)
                    for i in range(2):
                        k = 2 * (q0 + j) + i
                        if i or j:
                            pool.wait_ge(prep_sum, k)
                        g.tensor_tensor(accA[:, :], accA[:, :], sq[:, j % 2, i, :], ALU.add).then_inc(prep_sum, 1)

            sum_prep("pw1", 1)
            g.memset(w_if[:, :, :], 0.0).then_inc(w_if_ready, 1)
            pool.wait_ge(w_if_ready, 1)
            with nc.allow_non_contiguous_dma(reason="gate weights and states of a few bytes a row"):
                pool.dma_start(w_if[:, :, 0:H], mlstm_w_i[0].rearrange("(c p) h -> p c h", p=P)).then_inc(gates_in, 16)
                pool.dma_start(w_if[:, :, 32:32 + H], mlstm_w_f[0].rearrange("(c p) h -> p c h", p=P)).then_inc(gates_in, 16)
                pool.dma_start(b_gate[:, 0:1], mlstm_b_i.rearrange("l h -> h l")).then_inc(gates_in, 16)
                pool.dma_start(b_gate[:, 1:2], mlstm_b_f.rearrange("l h -> h l")).then_inc(gates_in, 16)
                pool.dma_start(m0[:, :], state_m[0].rearrange("b h -> h b")).then_inc(gates_in, 16)
            pool.dma_start(n0_rows[:, :], state_n[0].rearrange("b h k -> (b h) k")).then_inc(gates_in, 16)
            g.memset(mask_p[:, :], 0.0)
            g.memset(mask_s[:, :], 0.0)
            g.memset(seg[:, :], 1.0).then_inc(masks_ready, 1)
            pool.wait_ge(masks_ready, 1)
            g.affine_select(out=mask_p[:, :], in_=mask_p[:, :], compare_op=ALU.is_ge, fill=BIG, base=0,
                            pattern=[[1, TP]], channel_multiplier=-1)
            g.affine_select(out=mask_s[:, :], in_=mask_s[:, :], compare_op=ALU.is_ge, fill=BIG, base=0,
                            pattern=[[1, TS]], channel_multiplier=-1)
            g.affine_select(out=seg[:, :], in_=seg[:, :], compare_op=ALU.is_ge, fill=0.0, base=0,
                            pattern=[[-L, B]], channel_multiplier=1).then_inc(masks_ready, 1)
            pool.wait_ge(masks_ready, 2)
            g.affine_select(out=mask_s[:, :], in_=mask_s[:, :], compare_op=ALU.is_ge, fill=BIG, base=0,
                            pattern=[[-L, B], [0, L]], channel_multiplier=1)
            last = g.affine_select(out=seg[:, :], in_=seg[:, :], compare_op=ALU.is_ge, fill=0.0, base=L - 1,
                                   pattern=[[L, B]], channel_multiplier=-1)
            last.then_inc(masks_ready, 1)
            pool.wait_ge(stat_root, 2)
            g.memset(accA[:, :], 0.0).then_inc(conv_sum, 1)
            g.memset(accB[:, :], 0.0).then_inc(conv_sum, 1)
            pool.wait_ge(vec_ready, 2)
            steps = 1 + 2 * W

            def step(ins):
                ins.then_inc(smp_step, 1)

            def sample_conv(q, n):
                two = bass.ds(q * 2, 2)
                pool.wait_ge(banks_read, q + 1)
                g.tensor_copy(u_pair[:, 0:n, :, :], u_smp[:, bass.ds(q * 2, n), :, :])
                taps = vcol[:, 2 * P:2 * P + n_wdw].rearrange("p (j c) -> p j c", c=C)
                g.tensor_copy(w_pair[:, :, :], taps[:, :, two])
                step(g.tensor_copy(b_pair[:, :], vcol[:, bass.ds(q * 2 + v_at["b_dw"], 2)]))

                by_seq = lambda ap: ap.rearrange("p c (b t) -> p c b t", b=B)
                wide = lambda ap: ap.rearrange("p (c a b) -> p c a b", a=1, b=1).broadcast_to([P, n, B, L])
                y = by_seq(y_pair[:, 0:n, :])
                for j in range(W + 1):
                    product = lambda k: by_seq(prod[:, k % 2, 0:n, :])
                    if j < W:
                        pool.wait_ge(smp_step, q * steps + (2 * j if j > 1 else 1))
                        step(g.tensor_tensor(product(j), u_pair[:, 0:n, :, j:j + L], wide(w_pair[:, j, 0:n]), ALU.mult))
                    if j > 0:
                        pool.wait_ge(smp_step, q * steps + 2 * j)
                        step(g.tensor_tensor(y, product(j - 1), wide(b_pair[:, 0:n]) if j == 1 else y, ALU.add))
                pool.wait_ge(smp_step, q * steps + (2 * W + 1))
                g.tensor_copy(branch[:, bass.ds(q * 2, n), TP:T], y_pair[:, 0:n, :]).then_inc(smp_out, 1)

            def conv_sums(q):
                pool.wait_ge(smp_out, q + 1)
                for i in range(2):
                    c = q * 2 + i
                    pool.wait_ge(conv_sq, q * 2 + (i + 1))
                    pool.wait_ge(conv_sum, q * 4 + (2 * i + 2))
                    g.tensor_tensor(accA[:, :], accA[:, :], branch[:, c, :], ALU.add).then_inc(conv_sum, 1)
                    g.tensor_tensor(accB[:, :], accB[:, :], sq[:, 0, i, :], ALU.add).then_inc(conv_sum, 1)

            last_q = C // 2 - 1
            with pool.Fori(0, last_q) as q:
                sample_conv(q, 2)
                conv_sums(q)
            sample_conv(last_q, 1)
            conv_sums(last_q)

            pool.wait_ge(u_copied, 2 * C // 4)
            for b in range(B):
                pool.dma_start(conv_sample[0, b, TAIL - L:TAIL, :], u_rows[b * L:(b + 1) * L, 0, :]).then_inc(u_out, 16)
            pool.dma_start(conv_prompt[0, 0, :, :], u_rows[0:TAIL, 1, :]).then_inc(u_out, 16)

            pool.wait_ge(ln_step, 1)
            sum_prep("up0a", 2)
            sum_prep("qkv", 3)
            pool.dma_start(C0[:, :, :], state_C[0, :, 0, :, :].rearrange("b k v -> k b v")).then_inc(C0_in, 16)
            g.memset(qw_seq[:, :, :], 0.0)
            g.memset(keep_row[:, :], 1.0)
            g.memset(cut_row[:, :], 0.0).then_inc(masks_ready, 1)
            pool.wait_ge(masks_ready, 4)
            g.memset(keep_row[:, 0:1], 0.0)
            g.memset(keep_row[:, TP:T:L], 0.0)
            g.memset(cut_row[:, 0:1], BIG)
            g.memset(cut_row[:, TP:T:L], BIG).then_inc(masks_ready, 1)

            pool.wait_ge(row_dve, M_STEPS)
            with nc.allow_non_contiguous_dma(reason="64 stabilisers"):
                pool.dma_start(m_prompt.rearrange("l b h -> h (l b)"), m_row[:, TP - 1:TP]).then_inc(m_out, 16)
                pool.dma_start(m_sample[0].rearrange("b h -> h b"), m_row[:, TP + L - 1:T:L]).then_inc(m_out, 16)

            def states(h, last):
                pool.wait_ge(C_new, h * B + B)
                pool.wait_ge(Cp_read, h + 1)
                pool.dma_start(C_prompt[0, 0, bass.ds(h, 1), :, :].rearrange("h k v -> k (h v)"), Cn_prm[:, 0:DV]).then_inc(Cp_out, 16)
                pool.dma_start(C_sample[0, :, bass.ds(h, 1), :, :].rearrange("b h k v -> k (b h) v"), C0[:, :, :]).then_inc(C_out, 16)
                pool.wait_ge(Cp_out, h * 16 + 16)
                pool.wait_ge(C_out, h * 16 + 16)
                if not last:
                    pool.dma_start(C0[:, :, :], state_C[0, :, bass.ds(h + 1, 1), :, :].rearrange("b h k v -> k (b h) v")).then_inc(C0_in, 16)

            with pool.Fori(0, H - 1) as h:
                states(h, False)
            states(H - 1, True)
            sum_prep("up1a", 4)

            pool.wait_ge(n_copied, 1)
            pool.dma_start(n_sample[0].rearrange("b h k -> (b h) k"), vrows[0:B * H, 0, :]).then_inc(stored, 16)
            pool.dma_start(n_prompt[0].rearrange("b h k -> (b h) k"), vrows[B * H:B * H + H, 0, :]).then_inc(stored, 16)
            pool.wait_ge(stat_inv, POST_K[-1])
            for j in range(1, C // 2):
                scale_pair("end", j)
            pool.wait_ge(Cp_out, 16 * H)
            pool.wait_ge(C_out, 16 * H)
            pool.wait_ge(m_out, 32)
            pool.wait_ge(u_out, 16 * (B + 1))
            pool.wait_ge(stored, 16 * 3)

        def window(p, w, split, before):
            fixed = isinstance(w, int)
            for j in range(p.units):
                for f in before.get(j, []):
                    f()
                k = j + AHEAD
                if p is ph["pw1"] and not (fixed and w * p.units + k >= UNSPLIT):
                    continue
                if fixed:
                    u = w * p.units + k
                    q, r = p, u
                    if u >= p.units * p.groups:
                        if p.name not in follows:
                            continue
                        q, r = follows[p.name], u - p.units * p.groups
                    split(q, r // SLOTS, (q.unit0 + r) % SLOTS, q.unit0 + r)
                else:
                    split(p, w * (p.units // SLOTS) + k // SLOTS, k % SLOTS, w * p.units + (p.unit0 + k))
            for f in before.get(p.units, []):
                f()

        @block.scalar
        def _(act):
            s = nc.scalar

            def split(p, quad, slot, n):
                act.wait_ge(raw_in[slot], landed(p, quad, slot))
                if not isinstance(n, int) or n >= UNSPLIT + SLOTS:
                    act.wait_ge(units_used, n - (SLOTS - 1))
                s.activation(hi[:, slot, :, :], raw[:, slot, :, :], ACT.Copy).then_inc(hi_done, 1)

            def stat(k, *pieces):
                act.wait_ge(stat_sum, k)
                for src, dst in pieces:
                    last = s.activation(dst, src, ACT.Sqrt, bias=eps[:, 0:1], scale=1.0 / D)
                    last.then_inc(stat_root, 1)

            def squares(p, local, group):
                b = bank_of(group)
                for m in range(BANKS):
                    chunk = local * BANKS + m
                    written = br_out if m < BANKS - 1 else banks_read
                    if p.name in ("pw2", "out"):
                        wait_bank(act, p, local, m)
                        if p.name == "pw2":
                            ins = s.activation(branch[:, chunk, :], PS[:, b + m, 0:T], ACT.Identity, bias=vec("b_pw2", chunk))
                        else:
                            ins = s.activation(branch[:, chunk, :], PS[:, b + m, 0:T], ACT.Copy)
                        ins.then_inc(written, 1)
                    act.wait_ge(written, out_count(p, local) + (m + 1) if m < BANKS - 1 else group + 1)
                    act.wait_ge(br_acc, acc_count(p, local, max(0, m - 1)))
                    s.activation(sq[:, 0, m % 2, :], branch[:, chunk, :], ACT.Square).then_inc(br_sq, 1)

            def plain_out(p, local, group):
                wait_bank(act, p, local, BANKS - 1)
                b = bank_of(group)
                s.activation(branch[:, bass.ds(local * BANKS, BANKS), :], PS[:, bass.ds(b, BANKS), 0:T],
                             ACT.Copy).then_inc(banks_read, 1)

            def up_first_half(e):
                act.wait_ge(up_gate, e + 1)
                s.activation(tA[:, :, :], tA[:, :, :], ACT.Silu).then_inc(up_silu, 1)

            def up_second_half(e, chunk):
                act.wait_ge(up_prod, e + 1)
                s.activation(hh[:, bass.ds(chunk, 2), :], tB[:, :, :], ACT.Copy).then_inc(up_hi, 1)

            def glu(local):
                act.wait_ge(glu_in, local + 1)
                for i in range(2):
                    s.activation(tB[:, i, :], tB[:, i, :], ACT.Sigmoid,
                                 bias=vec("b_pw1", local * 2 + (C + i))).then_inc(glu_sig, 1)

            last_group = ph["pw1"].groups - 1

            def conv_squares(local):
                for i in range(2):
                    c = local * 2 + i
                    act.wait_ge(conv_step, local * (2 * W) + ((3 if local is last_group else 2) * W + 1))
                    act.wait_ge(smp_out, local + 1)
                    act.wait_ge(conv_sum, local * 4 + 2)
                    s.activation(sq[:, 0, i, :], branch[:, c, :], ACT.Square).then_inc(conv_sq, 1)

            def prep(name, j):
                q = C // 2 * prep_no[name] + j
                if name in ("pw1", "up0a", "qkv", "up1a"):
                    layer_norm = {"pw1": "mix_pre0", "up0a": "ffn_pre0", "qkv": "mix_pre1", "up1a": "ffn_pre1"}[name]
                    act.wait_ge(prep_front, q + 1)
                    k = C // 2 * sq_preps.index(name) + j
                    for c in (2 * j, 2 * j + 1):
                        last = s.activation((xg if name == "pw1" else xh)[:, c, :], x[:, c, :], ACT.Copy,
                                            scale=vec(layer_norm, c))
                    last.then_inc(prep_hi, 1)
                    if k >= 2:
                        act.wait_ge(prep_sum, 2 * k - 2)
                    s.activation(sq[:, j % 2, :, :], x[:, 2 * j:2 * j + 2, :], ACT.Square).then_inc(prep_sq, 1)
                elif name == "pw2":
                    act.wait_ge(prep_front, q + 1)
                    for c in (2 * j, 2 * j + 1):
                        last = s.activation(branch[:, c, :], branch[:, c, :], ACT.Silu, bias=vec("ln_b", c),
                                            scale=vec("ln_g", c))
                    last.then_inc(prep_act, 1)
                    act.wait_ge(prep_act, j + 1)
                    s.activation(xh[:, 2 * j:2 * j + 2, :], branch[:, 2 * j:2 * j + 2, :], ACT.Copy).then_inc(prep_hi, 1)
                elif name == "out":
                    act.wait_ge(prep_front, q + 1)
                    s.activation(xh[:, 2 * j:2 * j + 2, :], hn[:, 2 * j:2 * j + 2, :], ACT.Copy).then_inc(prep_hi, 1)

            def preps(name, then=()):
                out = {j: [lambda j=j: prep(name, j)] for j in range(C // 2)}
                out[C // 2] = list(then)
                return out

            def stat_rx(k, group):
                b = BANKS * (group % 2)
                cut = 512 - T
                stat(k, (PS[:, b, T:512], root[:, 0:cut]), (PS[:, b + 1, T:2 * T - cut], root[:, cut:T]))

            for r, n, k, src in vec_dmas:
                act.dma_start(vrows[r:r + n, k, :], src).then_inc(vec_in, 16)
            wdw = conv_w_dw[0].rearrange("j (c p) -> (j c) p", p=P)
            for k in range(4):
                n = min(P, n_wdw - k * P)
                act.dma_start(wdw_rows[0:n, k, :], wdw[k * P:k * P + n, :]).then_inc(wdw_in, 16)

            act.wait_ge(consts_ready, 5)
            act.wait_ge(vec_ready, 1)
            first = ph["pw1"]

            def cache_turn(j):
                act.wait_ge(cache_turned, j + 1)
                for i in range(2):
                    last = s.activation(u_smp[:, 2 * j + i, :, 0:TAIL], PS[:, 4 + j % 4, i * B * TAIL:(i + 1) * B * TAIL].rearrange(
                        "p (b t) -> p b t", b=B), ACT.Copy)
                last.then_inc(cache_ready, 1)

            before = preps("pw1", [lambda: stat_rx(1, 0)])
            for j in range(C // 2):
                before[j].append(lambda j=j: cache_turn(j))
            window(first, 0, split, before)
            p = first
            with act.Fori(1, p.groups - 1) as w:
                window(p, w, split, {0: [lambda: glu(w - 1)], p.units: [lambda: conv_squares(w - 1)]})
            w = p.groups - 1
            window(p, w, split, {0: [lambda: glu(w - 1)]})

            p = ph["pw2"]

            def u_copies():
                act.wait_ge(banks_read, p.group0)
                for b in range(B):
                    last = s.activation(u_new[:, :, b * L:(b + 1) * L], u_smp[:, :, b, TAIL:TAIL + L], ACT.Copy)
                last.then_inc(u_packed, 1)
                for half in range(2):
                    for k in range(C // 4):
                        act.wait_ge(u_turned, half * (C // 4) + k + 1)
                        n = TS if half == 0 else TAIL
                        bank = (k + BANKS * (1 - half) + BANKS * (p.group0 % 2)) % 8
                        s.activation(u_rows[0:n, half, 512 * k:512 * (k + 1)], PS[0:n, bank, :], ACT.Copy).then_inc(u_copied, 1)

            def ln_root():
                act.wait_ge(ln_step, LN_VAR)
                s.activation(root[:, :], root[:, :], ACT.Sqrt, bias=eps[:, 1:2]).then_inc(stat_root, 1)

            before = preps("pw2")
            before[0] = [lambda: glu(first.groups - 1), lambda: conv_squares(first.groups - 2), u_copies,
                         lambda: conv_squares(first.groups - 1), ln_root] + before[0]
            window(p, 0, split, before)
            for w in range(1, p.groups):
                window(p, w, split, {0: [lambda: squares(p, w - 1, w + (p.group0 - 1))]})

            def ffn(l, k_stat, prev):
                a, da, b, db = (ph[f"{n}{l}{s_}"] for s_ in "ab" for n in ("up", "down"))
                before = preps(f"up{l}a", [lambda: stat_rx(k_stat + 1, a.group0)])
                bank = BANKS * ((a.group0 - 1) % 2)
                before[0] = [lambda: squares(prev, prev.groups - 1, a.group0 - 1),
                             lambda: stat(k_stat, (PS[:, bank, 0:T], root[:, :]))] + before[0]
                window(a, 0, split, before)
                for up, down, start in ((a, da, 0), (b, db, 0)):
                    e0 = up_first[up.name]

                    def up_window(w):
                        return {0: [lambda: up_first_half(w + (e0 - 1))], 1: [lambda: up_second_half(w + (e0 - 1), w * 2 - 2)]}

                    if up is b:
                        window(b, 0, split, {0: [lambda: plain_out(da, da.groups - 1, da.group0 + da.groups - 1)]})
                    with act.Fori(1, up.groups - 1) as w:
                        window(up, w, split, up_window(w))
                    window(up, up.groups - 1, split, up_window(up.groups - 1))
                    window(down, 0, split, up_window(up.groups))
                    for w in range(1, down.groups):
                        f = plain_out if down is da else squares
                        window(down, w, split, {0: [lambda: f(down, w - 1, down.group0 + w - 1)]})

            act.wait_ge(u_out, 16 * (B + 1))
            ffn(0, 3, ph["pw2"])

            p = ph["qkv"]

            def row_gates():
                act.wait_ge(row_dve, 4)
                s.activation(f_abs[:, :], f_abs[:, :], ACT.Exp, scale=-1.0).then_inc(row_act, 1)
                act.wait_ge(row_act, 1)
                s.activation(f_abs[:, :], f_abs[:, :], ACT.Ln, bias=1.0).then_inc(row_act, 1)
                act.wait_ge(row_dve, M_STEPS)
                s.activation(rows[:, T + TS:2 * T + TS], m_row[:, :], ACT.Exp, scale=-1.0)
                act.wait_ge(row_dve, M_STEPS + 3)
                s.activation(rows[:, T:T + TS], rows[:, T:T + TS], ACT.Exp)
                s.activation(gr_row[:, :], gr_row[:, :], ACT.Exp).then_inc(row_act, 1)

            def cell_top(h):
                act.wait_ge(decay_in, h + 1)
                s.activation(prob[:, :], prob[:, :], ACT.Exp)
                s.activation(prob_s[:, :], prob_s[:, :], ACT.Exp).then_inc(decay_exp, 1)
                act.wait_ge(kv_turned, h + 1)
                s.activation(v_tok[:, 0:2, :], PS[:, 5, :].rearrange("p (t v) -> p t v", t=2), ACT.Copy).then_inc(v_ready, 1)

            def cell_den(h):
                act.wait_ge(inter_done, h + 1)
                s.activation(inter[:, :], PS[0:TS, 6, 0:DV], ACT.Copy).then_inc(inter_ready, 1)
                act.wait_ge(den_done, h + 1)
                s.activation(root[:, :], PS[:, 6, 0:T], ACT.Abs).then_inc(den_abs, 1)
                act.wait_ge(hq_ready, h + 1)
                s.activation(sq[:, 0, :, :], hq[:, :, :], ACT.Square).then_inc(hq_sq, 1)

            def cell_norm(h):
                act.wait_ge(hq_sum, h + 1)
                s.activation(root[:, :], PS[:, 6, 0:T], ACT.Ln, bias=eps[:, 0:1], scale=1.0 / DV).then_inc(hq_ln, 1)
                act.wait_ge(hq_ln, h + 1)
                s.activation(root[:, :], root[:, :], ACT.Exp, scale=-0.5).then_inc(hq_rs, 1)
                act.wait_ge(Cp_done, h + 1)
                s.activation(Cn_prm[:, :], PS[:, 4, 0:DV + B + 1], ACT.Copy).then_inc(Cp_read, 1)

            def cell_before(h):
                return {1: [lambda: cell_top(h)], 3: [lambda: cell_den(h)], 4: [lambda: cell_norm(h)]}

            before = preps("qkv", [lambda: stat_rx(6, p.group0), row_gates])
            bank = BANKS * ((p.group0 - 1) % 2)
            before[0] = [lambda: squares(ph["down0b"], ph["down0b"].groups - 1, p.group0 - 1),
                         lambda: stat(5, (PS[:, bank, 0:T], root[:, :]))] + before[0]
            window(p, 0, split, before)
            with act.Fori(1, p.groups) as w:
                window(p, w, split, cell_before(w - 1))
            p = ph["o"]
            window(p, 0, split, cell_before(H - 1))

            def o_gates(local):
                act.wait_ge(banks_read, ph["o"].group0 + local + 1)
                s.activation(branch[:, bass.ds(local * BANKS, BANKS), :], branch[:, bass.ds(local * BANKS, BANKS), :],
                             ACT.Sigmoid).then_inc(o_gate, 1)

            for w in range(1, p.groups):
                window(p, w, split, {0: [lambda: o_gates(w - 1)]})
            p = ph["out"]
            before = preps("out")
            before[0] = [lambda: o_gates(C // 4 - 1)] + before[0]
            window(p, 0, split, before)
            for w in range(1, p.groups):
                window(p, w, split, {0: [lambda: squares(p, w - 1, w + (p.group0 - 1))]})
            act.wait_ge(C_out, 16 * H)
            act.wait_ge(Cp_out, 16 * H)
            ffn(1, 7, ph["out"])

            db = ph["down1b"]
            squares(db, db.groups - 1, db.group0 + db.groups - 1)
            stat(9, (PS[:, BANKS * ((db.group0 + db.groups - 1) % 2), 0:T], root[:, :]))
            for k in range(C // 4):
                for t in range(3):
                    n = P if t < 2 else TS
                    act.wait_ge(y_turned, 3 * k + t + 1)
                    s.activation(y_rows[0:n, t, 512 * k:512 * (k + 1)], PS[0:n, (3 * k + t) % 8, :], ACT.Copy).then_inc(y_copied, 1)

        @block.vector
        def _(dve):
            v = nc.vector
            done = [None]

            def split(p, quad, slot, n):
                dve.wait_ge(hi_done, n + (1 - UNSPLIT))
                v.tensor_tensor(lo[:, slot, :, :], raw[:, slot, :, :], hi[:, slot, :, :].bitcast(F32),
                                ALU.subtract).then_inc(lo_done, 1)
                done[0] = n + (1 - UNSPLIT)

            def fence():
                dve.wait_ge(lo_done, done[0])

            def wide(t, n=2):
                return t[:, :].rearrange("p (a t) -> p a t", a=1).broadcast_to([P, n, T])

            def add_squares(p, local):
                for m in range(BANKS):
                    dve.wait_ge(br_sq, local * BANKS + (sq_no[p.name] * C + m + 1))
                    dve.wait_ge(br_acc, acc_count(p, local, m))
                    v.tensor_tensor(acc[:, :], acc[:, :], sq[:, 0, m % 2, :], ALU.add).then_inc(br_acc, 1)

            def add_branch(p, local, group):
                b = bank_of(group)
                for m in range(BANKS):
                    chunk = local * BANKS + m
                    wait_bank(dve, p, local, m)
                    v.tensor_tensor(branch[:, chunk, :], branch[:, chunk, :], PS[:, b + m, 0:T],
                                    ALU.add).then_inc(br_out if m < BANKS - 1 else banks_read, 1)
                add_squares(p, local)

            def clear_acc():
                fence()
                v.memset(acc[:, :], 0.0).then_inc(br_acc, 1)

            def inverse(k, dst):
                dve.wait_ge(stat_root, ROOTS[k])
                v.reciprocal(dst[:, :], root[:, :]).then_inc(stat_inv, 1)
                dve.wait_ge(stat_inv, k)

            def up_part1(p, local):
                b = bank_of(local + p.group0)
                wait_bank(dve, p, local, 1)
                fence()
                v.tensor_tensor(tA[:, :, :], PS[:, bass.ds(b, 2), 0:T], wide(rx), ALU.mult).then_inc(up_gate, 1)
                wait_bank(dve, p, local, 3)
                v.tensor_tensor(tB[:, :, :], PS[:, bass.ds(b + 2, 2), 0:T], wide(rx), ALU.mult).then_inc(banks_read, 1)

            def up_part2(group, e):
                dve.wait_ge(up_silu, e + 1)
                dve.wait_ge(banks_read, group + 1)
                v.tensor_tensor(tB[:, :, :], tB[:, :, :], tA[:, :, :], ALU.mult).then_inc(up_prod, 1)

            def up_part3(e, chunk):
                dve.wait_ge(up_hi, e + 1)
                v.tensor_tensor(hl[:, bass.ds(chunk, 2), :], tB[:, :, :], hh[:, bass.ds(chunk, 2), :].bitcast(F32),
                                ALU.subtract).then_inc(h_ready, 1)

            def glu_in_part(local, group):
                b = bank_of(group)
                dve.wait_ge(conv_step, local * (2 * W) + 1)
                wait_bank(dve, ph["pw1"], local, 1)
                v.tensor_tensor(tA[:, :, :], PS[:, bass.ds(b, 2), 0:T], wide(rx), ALU.mult)
                wait_bank(dve, ph["pw1"], local, 3)
                v.tensor_tensor(tB[:, :, :], PS[:, bass.ds(b + 2, 2), 0:T], wide(rx), ALU.mult).then_inc(glu_in, 1)

            def glu_out_part(local):
                for i in range(2):
                    c = local * 2 + i
                    dve.wait_ge(glu_sig, local * 2 + (i + 1))
                    v.scalar_tensor_tensor(out=u_prm[:, c, TAIL:TAIL + TP], in0=tA[:, i, 0:TP], scalar=vec("b_pw1", c),
                                           in1=tB[:, i, 0:TP], op0=ALU.add, op1=ALU.mult)
                    last = v.scalar_tensor_tensor(
                        out=u_smp[:, c, :, TAIL:TAIL + L], in0=tA[:, i, TP:T].rearrange("p (b t) -> p b t", b=B),
                        scalar=vec("b_pw1", c), in1=tB[:, i, TP:T].rearrange("p (b t) -> p b t", b=B),
                        op0=ALU.add, op1=ALU.mult)
                last.then_inc(banks_read, 1)

            def conv_taps(local, group, taps, last=False):
                if taps[0] == 0:
                    dve.wait_ge(banks_read, group + 1)
                sums = [(0, True), (1, True)] + [(1, False)] * last
                for j in taps:
                    for n, (i, prompt) in enumerate(sums):
                        c = local * 2 + i
                        w_j = vec("w_dw", c + j * C)
                        if prompt:
                            out, u = branch[:, c, 0:TP], u_prm[:, c, j:j + TP]
                        else:
                            out, u = branch[:, c, TP:T].rearrange("p (b t) -> p b t", b=B), u_smp[:, c, :, j:j + L]
                        if j == 0:
                            v.tensor_scalar(out, u, w_j, vec("b_dw", c), ALU.mult, ALU.add).then_inc(conv_step, 1)
                        else:
                            dve.wait_ge(conv_step, local * (2 * W) + (len(sums) * (j - 1) + n + 2))
                            v.scalar_tensor_tensor(out=out, in0=u, scalar=w_j, in1=out, op0=ALU.mult,
                                                   op1=ALU.add).then_inc(conv_step, 1)

            def conv_before(local, group, n=ph["pw1"].units):
                step = -(-W // n)
                out = {k: [lambda k=k: conv_taps(local, group, range(k * step, min(W, (k + 1) * step)))] for k in range(n)}
                out[0] = [lambda: glu_in_part(local, group), lambda: glu_out_part(local)] + out[0]
                return out

            def prep_front_part(name, j):
                q = C // 2 * prep_no[name] + j
                two = slice(2 * j, 2 * j + 2)
                if name == "pw1":
                    for c in (2 * j, 2 * j + 1):
                        dve.wait_ge(x_turned, c + 1)
                        last = v.tensor_copy(x[:, c, :], PS[:, 4 + c % 4, 0:T])
                    last.then_inc(prep_front, 1)
                elif name in ("up0a", "qkv", "up1a", "end"):
                    post = {"up0a": "mix_post0", "qkv": "ffn_post0", "up1a": "mix_post1", "end": "ffn_post1"}[name]
                    k = posts.index(name)
                    if j == 0:
                        v.tensor_tensor(branch[:, two, :], branch[:, two, :], wide(rp), ALU.mult).then_inc(prep_scaled, 1)
                        dve.wait_ge(prep_scaled, k + 1)
                    else:
                        dve.wait_ge(pair_scaled, k * (C // 2 - 1) + j)
                    for c in (2 * j, 2 * j + 1):
                        last = v.scalar_tensor_tensor(out=x[:, c, :], in0=branch[:, c, :], scalar=vec(post, c),
                                                      in1=x[:, c, :], op0=ALU.mult, op1=ALU.add)
                    last.then_inc(prep_front, 1)
                elif name == "pw2":
                    v.tensor_tensor(branch[:, two, :], branch[:, two, :], wide(tA[:, 0, :]), ALU.subtract).then_inc(ln_step, 1)
                    dve.wait_ge(ln_step, LN_VAR + j + 1)
                    v.tensor_tensor(branch[:, two, :], branch[:, two, :], wide(rp), ALU.mult).then_inc(prep_front, 1)
                elif name == "out":
                    dve.wait_ge(o_gate, j // 2 + 1)
                    v.tensor_tensor(hn[:, two, :], hn[:, two, :], branch[:, two, :], ALU.mult).then_inc(prep_front, 1)

            def prep_back_part(name, j):
                k = C // 2 * prep_no[name] + j
                dve.wait_ge(prep_hi, k + 1)
                two = slice(2 * j, 2 * j + 2)
                if name in ("pw2", "out"):
                    src = branch if name == "pw2" else hn
                    v.tensor_tensor(xl[:, two, :], src[:, two, :], xh[:, two, :].bitcast(F32), ALU.subtract).then_inc(prep_lo, 1)
                else:
                    pre = {"pw1": "mix_pre0", "up0a": "ffn_pre0", "qkv": "mix_pre1", "up1a": "ffn_pre1"}[name]
                    for c in (2 * j, 2 * j + 1):
                        last = v.scalar_tensor_tensor(out=xl[:, c, :], in0=x[:, c, :], scalar=vec(pre, c),
                                                      in1=xh[:, c, :].bitcast(F32), op0=ALU.mult, op1=ALU.subtract)
                    last.then_inc(prep_lo, 1)

            def preps(name, first=(), then=()):
                n = C // 2
                out = {j: [lambda j=j: prep_back_part(name, j)] if name != "pw1" else [] for j in range(n)}
                if name != "pw1":
                    for j in range(n):
                        out[max(0, j - 1)].insert(0 if j == 0 else len(out[j - 1]), lambda j=j: prep_front_part(name, j))
                out[0] = list(first) + out[0]
                out[n] = out.get(n, []) + list(then)
                return out

            def vec_columns(k):
                dve.wait_ge(vec_turned, k + 1)
                n = P + vec_rows[1] if k == 0 else n_wdw
                at_ = 0 if k == 0 else 2 * P
                v.tensor_copy(vcol[:, at_:at_ + n], PS[:, k, 0:n]).then_inc(vec_ready, 1)

            vec_columns(0)
            first = ph["pw1"]
            for j in range(C // 2):
                prep_front_part("pw1", j)
            vec_columns(1)
            dve.wait_ge(vec_ready, 2)

            def zero_past():
                dve.wait_ge(x_turned, C)
                v.memset(u_prm[:, :, 0:TAIL], 0.0).then_inc(conv_step, 1)

            window(first, 0, split, preps("pw1", then=[zero_past, lambda: inverse(1, rx)]))
            p = first
            dve.wait_ge(cache_ready, C // 2)
            with dve.Fori(1, p.groups - 1) as w:
                window(p, w, split, conv_before(w - 1, w + (p.group0 - 1)))
            w = p.groups - 1
            window(p, w, split, conv_before(w - 1, w + (p.group0 - 1), p.units - AHEAD))

            p = ph["pw2"]

            def last_conv():
                g = first.groups - 1
                glu_in_part(g, g)
                glu_out_part(g)
                conv_taps(g, g, range(W), last=True)

            def ln_stats():
                b = BANKS * ((p.group0 - 1) % 2)
                dve.wait_ge(stat_sum, 2)
                v.tensor_scalar(tA[:, 0, :], PS[:, b, 0:T], 1.0 / D, None, ALU.mult).then_inc(ln_step, 1)
                dve.wait_ge(ln_step, 1)
                v.tensor_tensor(tA[:, 1, :], tA[:, 0, :], tA[:, 0, :], ALU.mult).then_inc(ln_step, 1)
                dve.wait_ge(ln_step, 2)
                v.scalar_tensor_tensor(out=root[:, :], in0=PS[:, b + 1, 0:T], scalar=1.0 / D, in1=tA[:, 1, :],
                                       op0=ALU.mult, op1=ALU.subtract).then_inc(ln_step, 1)
                inverse(2, rp)

            window(p, 0, split, preps("pw2", first=[last_conv, ln_stats], then=[lambda: clear_acc()]))

            def squares_window(p, w):
                return {0: [lambda: add_squares(p, w - 1)]}

            def looped(p, make):
                with dve.Fori(1, p.groups - 1) as w:
                    done[0] = w * p.units + (p.unit0 + AHEAD - UNSPLIT)
                    window(p, w, split, make(w))
                w = p.groups - 1
                done[0] = w * p.units + (p.unit0 + AHEAD - UNSPLIT)
                window(p, w, split, make(w))

            looped(p, lambda w: squares_window(p, w))

            def ffn(l, k_inv, prev):
                a, da, b, db = (ph[f"{n}{l}{s_}"] for s_ in "ab" for n in ("up", "down"))
                window(a, 0, split, preps(f"up{l}a", first=[lambda: add_squares(prev, prev.groups - 1),
                                                           lambda: inverse(k_inv, rp)],
                                          then=[lambda: inverse(k_inv + 1, rx)]))
                for up, down in ((a, da), (b, db)):
                    e0 = up_first[up.name]

                    def up_window(w):
                        group, e = w + (up.group0 - 1), w + (e0 - 1)
                        return {0: [lambda: up_part1(up, w - 1)], 1: [lambda: up_part2(group, e)],
                                2: [lambda: up_part3(e, w * 2 - 2)]}

                    if up is b:
                        window(b, 0, split, {})
                    looped(up, up_window)
                    last = up_window(up.groups)
                    if down is db:
                        last[3] = [lambda: clear_acc()]
                    window(down, 0, split, last)
                    for w in range(1, down.groups):
                        window(down, w, split, {} if down is da else {0: [lambda: add_branch(db, w - 1, db.group0 + w - 1)]})

            dve.wait_ge(u_out, 16 * (B + 1))
            ffn(0, 3, ph["pw2"])

            p = ph["qkv"]

            def steps():
                k = [0]

                def link(ins):
                    k[0] += 1
                    ins.then_inc(row_dve, 1)
                    dve.wait_ge(row_dve, k[0])

                f32 = slice(32, 32 + H)
                dve.wait_ge(gate_mm, 1)
                dve.wait_ge(masks_ready, 5)
                v.scalar_tensor_tensor(out=i_row[:, :], in0=PS[0:H, 6, 0:T], scalar=1.0, in1=rx[0:H, :], op0=ALU.mult, op1=ALU.mult)
                link(v.tensor_tensor(f_row[:, :], PS[f32, 6, 0:T], rx[f32, :], ALU.mult))
                v.tensor_scalar(i_row[:, :], i_row[:, :], b_gate[:, 0:1], None, ALU.add)
                link(v.tensor_scalar(f_row[:, :], f_row[:, :], b_gate[:, 1:2], None, ALU.add))
                link(v.tensor_scalar(f_min[:, :], f_row[:, :], 0.0, None, ALU.min))
                link(v.scalar_tensor_tensor(out=f_abs[:, :], in0=f_row[:, :], scalar=-1.0, in1=f_row[:, :], op0=ALU.mult, op1=ALU.max))
                dve.wait_ge(row_act, 2)
                link(v.tensor_tensor(f_row[:, :], f_min[:, :], f_abs[:, :], ALU.subtract))
                link(v.tensor_tensor_scan(b_row[:, :], keep_row[:, :], f_row[:, :], 0.0, ALU.mult, ALU.add))
                link(v.tensor_tensor(c_row[:, :], i_row[:, :], b_row[:, :], ALU.subtract))
                link(v.tensor_tensor_scan(cum_row[:, :], cut_row[:, :], c_row[:, :], 0.0, ALU.add, ALU.max))
                v.tensor_scalar(rows[:, 0:TP], cum_row[:, 0:TP], 0.0, None, ALU.max)
                m0_wide = m0[:, :].rearrange("h (b t) -> h b t", t=1).broadcast_to([H, B, L])
                by_seq = lambda ap: ap.rearrange("h (b t) -> h b t", b=B)
                link(v.tensor_tensor(by_seq(rows[:, TP:T]), by_seq(cum_row[:, TP:T]), m0_wide, ALU.max))
                link(v.tensor_tensor(m_row[:, :], b_row[:, :], rows[:, 0:T], ALU.add))
                assert k[0] == M_STEPS, k[0]
                link(v.tensor_tensor(by_seq(rows[:, T:T + TS]), m0_wide, by_seq(rows[:, TP:T]), ALU.subtract))
                link(v.tensor_scalar(gr_row[:, 0:TP], c_row[:, 0:TP], rows[:, TP - 1:TP], None, ALU.subtract))
                m_last = rows[:, TP + L - 1:T:L].rearrange("h (b t) -> h b t", t=1).broadcast_to([H, B, L])
                link(v.tensor_tensor(by_seq(gr_row[:, TP:T]), by_seq(c_row[:, TP:T]), m_last, ALU.subtract))
                dve.wait_ge(row_turned, 1)
                cols = lambda r, k: PS[0:r, 5, k:k + 3 * H].rearrange("p (t h) -> p t h", t=3)
                for k0, dst in ((0, c_tok), (3 * H, gr_tok)):
                    v.tensor_copy(dst[:, 0:2, :], cols(P, k0)[:, 0:2, :])
                    v.tensor_copy(dst[0:TS, 2, :], cols(TS, k0)[:, 2, :])
                v.tensor_copy(n0T[:, :], PS[:, 5, 6 * H:6 * H + B * H]).then_inc(row_cols, 1)
                dve.wait_ge(row_cols, 1)

            def w_if_scale():
                dve.wait_ge(gates_in, 16 * 6)
                g_pre = vcol[:, v_at["mix_pre1"]:v_at["mix_pre1"] + C].rearrange("p (c n) -> p c n", n=1).broadcast_to([P, C, 40])
                v.tensor_tensor(w_if[:, :, :], w_if[:, :, :], g_pre, ALU.mult).then_inc(w_if_ready, 1)

            w_if_scale()

            def head_out(h):
                fence()
                v.tensor_scalar(rows_h[:, :], rows[:, :], ident[0:H, bass.ds(h, 1)], None, ALU.mult).then_inc(head_rows, 1)

            def qk_out(h):
                wait_bank(dve, ph["qkv"], h, 0)
                v.scalar_tensor_tensor(out=qT[:, :], in0=PS[:, 0, 0:T], scalar=float(DK) ** -0.5, in1=rx[:, :],
                                       op0=ALU.mult, op1=ALU.mult)
                wait_bank(dve, ph["qkv"], h, 1)
                v.tensor_tensor(kT[:, :], PS[:, 1, 0:T], rx[:, :], ALU.mult)

            def v_out(h):
                for i in range(2):
                    wait_bank(dve, ph["qkv"], h, 2 + i)
                    last = v.tensor_tensor(vT[:, i, :], PS[:, 2 + i, 0:T], rx[:, :], ALU.mult)
                last.then_inc(banks_read, 1)

            def cell_top(h):
                dve.wait_ge(tables, h + 1)
                col = lambda t, n, r=P: t[0:r, n, bass.ds(h, 1)]
                v.scalar_tensor_tensor(out=prob[:, 0:TP], in0=mask_p[:, :], scalar=col(c_tok, 0), in1=PS[:, 6, 0:TP],
                                       op0=ALU.add, op1=ALU.subtract)
                v.scalar_tensor_tensor(out=prob[:, TP:TP + P], in0=mask_p[:, 0:P], scalar=col(c_tok, 1), in1=PS[:, 6, P:TP],
                                       op0=ALU.add, op1=ALU.subtract)
                v.scalar_tensor_tensor(out=prob_s[:, :], in0=mask_s[:, :], scalar=col(c_tok, 2, TS), in1=PS[0:TS, 6, TP:T],
                                       op0=ALU.add, op1=ALU.subtract).then_inc(decay_in, 1)
                v.tensor_copy(g_state[:, :], PS[:, 6, T + L - 1:T + TS:L])
                by_seq = lambda ap: ap.rearrange("p (b t) -> p b t", b=B)
                qw = bass.AP(tensor=qw_seq, offset=0, ap=[[B * TS, P], [TS + L, B], [1, L]])
                v.tensor_tensor(qw, by_seq(qT[:, TP:T]), by_seq(PS[:, 6, T:T + TS]), ALU.mult).then_inc(qw_ready, 1)
                dve.wait_ge(qw_ready, h + 1)
                n_head = n0T[:, :].rearrange("p (b h) -> p h b", b=B)[:, bass.ds(h, 1), :].rearrange("p h b -> p (h b)")
                v.tensor_tensor(by_seq(qn[:, :]), qw,
                                n_head.rearrange("p (b t) -> p b t", t=1).broadcast_to([P, B, L]), ALU.mult).then_inc(qn_ready, 1)
                dve.wait_ge(kv_turned, h + 1)
                v.tensor_scalar(kw[0:TS, 2, :], PS[0:TS, 6, T + TS:T + TS + P], col(gr_tok, 2, TS), None, ALU.mult).then_inc(kw_ready, 1)
                for t in range(2):
                    v.tensor_scalar(kw[:, t, :], PS[:, 4, t * P:(t + 1) * P], col(gr_tok, t), None, ALU.mult)
                v.tensor_copy(v_tok[0:TS, 2, :], PS[0:TS, 4, 2 * P:4 * P]).then_inc(kw_ready, 1)
                dve.wait_ge(kw_ready, h * 2 + 2)
                v.tensor_tensor(kw_seq[:, :, :], kw[0:TS, 2, :].rearrange("s (a k) -> s a k", a=1).broadcast_to([TS, B, DK]),
                                seg[:, :].rearrange("s (b a) -> s b a", a=1).broadcast_to([TS, B, DK]), ALU.mult).then_inc(kw_seq_ready, 1)
                dve.wait_ge(decay_exp, h + 1)
                dve.wait_ge(scores, h + 1)
                v.tensor_tensor(prob[:, :], prob[:, :], PS[:, 7, 0:3 * P], ALU.mult)
                v.tensor_tensor(prob_s[:, :], prob_s[:, :], PS[0:TS, 7, 3 * P:3 * P + TS], ALU.mult).then_inc(prob_ready, 1)

            def cell_den(h):
                dve.wait_ge(den_abs, h + 1)
                v.tensor_tensor(tC[:, 0, :], root[:, :], PS[:, 7, 0:T], ALU.max).then_inc(den_max, 1)
                dve.wait_ge(den_max, h + 1)
                v.reciprocal(tC[:, 1, :], tC[:, 0, :]).then_inc(den_inv, 1)
                dve.wait_ge(den_inv, h + 1)
                dve.wait_ge(num_done, h + 1)
                v.tensor_tensor(hq[:, :, :], PS[:, 4:6, 0:T], wide(tC[:, 1, :]), ALU.mult).then_inc(hq_ready, 1)

            def cell_norm(h):
                dve.wait_ge(hq_rs, h + 1)
                for i in range(2):
                    v.scalar_tensor_tensor(out=hn[:, h * 2 + i, :], in0=hq[:, i, :], scalar=vec("g_mh", h * 2 + i),
                                           in1=root[:, :], op0=ALU.mult, op1=ALU.mult)
                n_head = lambda t: t[:, 0:B * H].rearrange("p (b h) -> p h b", b=B)[:, bass.ds(h, 1), :].rearrange("p h b -> p (h b)")
                v.tensor_tensor(tC[:, 0, 0:B], n_head(n0T), g_state[:, :], ALU.mult).then_inc(n_scaled, 1)
                dve.wait_ge(n_scaled, h + 1)
                dve.wait_ge(Cp_read, h + 1)
                v.tensor_tensor(n_head(n_new), tC[:, 0, 0:B], Cn_prm[:, DV:DV + B], ALU.add)
                v.tensor_copy(n_new[:, bass.ds(h + B * H, 1)], Cn_prm[:, DV + B:DV + B + 1]).then_inc(n_done, 1)

            def cell_state(h, pair):
                dve.wait_ge(Cs_done, h * (B // 2) + (pair + 1))
                for i in range(2):
                    b = 2 * pair + i
                    v.scalar_tensor_tensor(out=C0[:, b, :], in0=C0[:, b, :], scalar=g_state[:, b:b + 1],
                                           in1=PS[:, 5 + 2 * (pair % 2), i * DV:(i + 1) * DV], op0=ALU.mult, op1=ALU.add).then_inc(C_new, 1)

            def cell_before(h, last=False, first_head=False):
                return {0: [lambda: v_out(h)] if not first_head else [], 1: [lambda: cell_top(h)], 3: [lambda: cell_den(h)],
                        4: [lambda: cell_norm(h)], 5: [lambda: cell_state(h, 0), lambda: cell_state(h, 1)],
                        6: [lambda: cell_state(h, 2)],
                        7: [lambda: cell_state(h, 3)] + ([] if last else [lambda: head_out(h + 1), lambda: qk_out(h + 1)])}

            before = preps("qkv", first=[lambda: add_branch(ph["down0b"], ph["down0b"].groups - 1, p.group0 - 1),
                                         lambda: inverse(5, rp)], then=[lambda: inverse(6, rx), lambda: qk_out(0), lambda: v_out(0), steps, lambda: head_out(0)])
            window(p, 0, split, before)
            window(p, 1, split, cell_before(0, first_head=True))
            with dve.Fori(2, p.groups) as w:
                done[0] = w * p.units + (p.unit0 + AHEAD - UNSPLIT)
                window(p, w, split, cell_before(w - 1))
            p = ph["o"]
            done[0] = p.unit0 + AHEAD - UNSPLIT
            window(p, 0, split, cell_before(H - 1, last=True))

            def o_out(local, group):
                four = slice(local * BANKS, (local + 1) * BANKS)
                wait_bank(dve, ph["o"], local, 3)
                b = bank_of(group) if local else 0
                v.tensor_tensor(branch[:, four, :], PS[:, b:b + BANKS, 0:T], wide(rx, BANKS), ALU.mult).then_inc(banks_read, 1)

            dve.wait_ge(n_turned, 1)
            v.tensor_copy(vrows[0:B * H + H, 0, :], PS[0:B * H + H, 7, 0:P]).then_inc(n_copied, 1)
            for w in range(1, p.groups):
                window(p, w, split, {0: [lambda: o_out(w - 1, p.group0 + w - 1)]})
            p = ph["out"]

            window(p, 0, split, preps("out", first=[lambda: o_out(C // 4 - 1, p.group0 - 1)],
                                      then=[lambda: clear_acc()]))
            looped(p, lambda w: squares_window(p, w))
            dve.wait_ge(C_out, 16 * H)
            dve.wait_ge(Cp_out, 16 * H)
            dve.wait_ge(m_out, 32)
            ffn(1, 7, ph["out"])

            db = ph["down1b"]
            add_branch(db, db.groups - 1, db.group0 + db.groups - 1)
            inverse(9, rp)
            for j in range(C // 2):
                prep_front_part("end", j)

        @block.tensor
        def _(pe):
            mm, turn = nc.tensor.matmul, nc.tensor.transpose

            def unit(p, g_bank, j, slot, quad, n, rhs_hi, rhs_lo):
                if p is ph["pw1"]:
                    pe.wait_ge(raw_in[slot], landed(p, quad, slot))
                else:
                    pe.wait_ge(lo_done, n + (1 - UNSPLIT))
                last_unit = j == p.units - 1
                for m in range(BANKS):
                    out = PS[:, g_bank + m, 0:T]
                    cols = slice(m * P, (m + 1) * P)
                    for kk in range(2):
                        k = 2 * j + kk
                        begin, end = k == 0, last_unit and kk == 1
                        if p is ph["pw1"]:
                            ins = mm(out, raw[:, slot, kk, cols], xg[:, k, :], start=begin, stop=end, skip_group_check=True)
                            continue
                        mm(out, hi[:, slot, kk, cols], rhs_hi[:, k, :], start=begin, stop=False, skip_group_check=True)
                        mm(out, hi[:, slot, kk, cols], rhs_lo[:, k, :], start=False, stop=False, skip_group_check=True)
                        ins = mm(out, lo[:, slot, kk, cols], rhs_hi[:, k, :], start=False, stop=end, skip_group_check=True)
                    if last_unit and m < BANKS - 1:
                        ins.then_inc(bank_done, 1)
                ins.then_inc(units_used, 1)

            def group(p, g, before=None, single=False, rep=0):
                before = before or {}
                glob = g + p.group0
                rhs = (hh, hl) if p.name[:4] == "down" else (xh, xl)
                b = 0 if single else bank_of(glob)
                if not isinstance(g, int) or glob >= 2:
                    pe.wait_ge(banks_read, glob if single else glob - 1)
                for j in range(p.units):
                    for f in before.get(j, []):
                        f()
                    u = rep * p.units + j
                    n = g * p.units + (p.unit0 + j)
                    unit(p, b, j, u % SLOTS, g * (p.units // SLOTS) + j // SLOTS, n, *rhs)
                for f in before.get(p.units, []):
                    f()

            def phase(p, first=None, single=False):
                start = 0
                if first is not None:
                    group(p, 0, first, single)
                    start = 1
                with pe.Fori(start, p.groups) as g:
                    group(p, g, None, single)

            def sum_over_features(out, src, **kw_):
                return mm(out, ones[:, :], src, skip_group_check=True, **kw_)

            def wait_preps(name, j):
                if name == "pw1":
                    pe.wait_ge(prep_hi, j + 1)
                else:
                    pe.wait_ge(prep_lo, C // 2 * (prep_no[name] - 1) + j + 1)

            def stat_rx(name, g):
                b = BANKS * (g % 2)
                cut = 512 - T
                pe.wait_ge(prep_sum, C * (sq_preps.index(name) + 1))
                sum_over_features(PS[:, b, T:512], accA[:, 0:cut], start=True, stop=True)
                sum_over_features(PS[:, b + 1, T:2 * T - cut], accA[:, cut:T], start=True, stop=True).then_inc(stat_sum, 1)

            def stat_post(no, g):
                pe.wait_ge(br_acc, (no + 1) * (C + 1))
                sum_over_features(PS[:, BANKS * ((g - 1) % 2), 0:T], acc[:, :], start=True, stop=True).then_inc(stat_sum, 1)

            def prep_windows(name, then=()):
                out = {j: [lambda j=j: wait_preps(name, j)] for j in range(C // 2)}
                out[C // 2] = list(then)
                return out

            pe.wait_ge(consts_ready, 5)
            pe.wait_ge(vec_in, 16 * len(vec_dmas))
            for k in range(2):
                ins = turn(PS[:, 0, k * P:k * P + vec_rows[k]], vrows[0:vec_rows[k], k, :], ident[0:vec_rows[k], 0:vec_rows[k]])
            ins.then_inc(vec_turned, 1)
            for c in range(C):
                if c % (C // 2) == 0:
                    pe.wait_ge(x_in[c // (C // 2)], 16 * 3)
                if c >= 4:
                    pe.wait_ge(prep_front, (c - 4) // 2 + 1)
                cols = slice(c * P, (c + 1) * P)
                for t in range(2):
                    turn(PS[:, 4 + c % 4, t * P:(t + 1) * P], x_rows[:, t, cols], ident[:, :])
                turn(PS[:, 4 + c % 4, TP:T], x_rows2[:, cols], ident[0:TS, 0:TS]).then_inc(x_turned, 1)
            pe.wait_ge(wdw_in, 16 * 4)
            for k in range(4):
                n = min(P, n_wdw - k * P)
                ins = turn(PS[:, 1, k * P:k * P + n], wdw_rows[0:n, k, :], ident[0:n, 0:n])
            ins.then_inc(vec_turned, 1)

            def cache_turn(j):
                if j == 0:
                    pe.wait_ge(cache_in, 16)
                    pe.wait_ge(prep_front, C // 2)
                if j >= 4:
                    pe.wait_ge(cache_ready, j - 3)
                half = B // 2 * TAIL
                for i in range(2):
                    c = 2 * j + i
                    for r in range(2):
                        ins = turn(PS[:, 4 + j % 4, (2 * i + r) * half:(2 * i + r + 1) * half], cache_rows[:, r, c * P:(c + 1) * P],
                                   ident[0:half, 0:half])
                ins.then_inc(cache_turned, 1)

            p = ph["pw1"]
            before = prep_windows("pw1", [lambda: stat_rx("pw1", 0)])
            for j in range(C // 2):
                before[j].append(lambda j=j: cache_turn(j))
            pe.wait_ge(vec_ready, 2)
            group(p, 0, before)
            pe.wait_ge(cache_ready, C // 2)
            group(p, 1)
            with pe.Fori(2, p.groups) as g:
                group(p, g)

            p = ph["pw2"]
            pe.wait_ge(banks_read, p.group0)
            pe.wait_ge(u_packed, 1)
            for half in range(2):
                for k in range(C // 4):
                    bank = (k + BANKS * (1 - half) + BANKS * (p.group0 % 2)) % 8
                    for i in range(4):
                        c = 4 * k + i
                        if half == 0:
                            ins = turn(PS[0:TS, bank, i * P:(i + 1) * P], u_new[:, c, :], ident[:, :])
                        else:
                            ins = turn(PS[0:TAIL, bank, i * P:(i + 1) * P], u_prm[:, c, TP:TP + TAIL], ident[:, :])
                    ins.then_inc(u_turned, 1)
            pe.wait_ge(conv_sum, 2 * C + 2)
            pe.wait_ge(u_copied, C // 2)
            b = BANKS * ((p.group0 - 1) % 2)
            sum_over_features(PS[:, b, 0:T], accA[:, :], start=True, stop=True)
            sum_over_features(PS[:, b + 1, 0:T], accB[:, :], start=True, stop=True).then_inc(stat_sum, 1)
            phase(p, prep_windows("pw2"))

            def ffn(l, no):
                a, da, b_, db = (ph[f"{n}{l}{s_}"] for s_ in "ab" for n in ("up", "down"))
                stat_post(no, a.group0)
                phase(a, prep_windows(f"up{l}a", [lambda: stat_rx(f"up{l}a", a.group0)]))

                def wait_h(up, j):
                    pe.wait_ge(h_ready, up_first[up.name] + j + 1)

                group(da, 0, {j: [lambda j=j: wait_h(a, j)] for j in range(da.units)})
                with pe.Fori(1, da.groups) as g:
                    group(da, g)
                phase(b_)
                with pe.Fori(0, db.groups // 2) as it:
                    group(db, it * 2, {j: [lambda j=j: wait_h(b_, j)] for j in range(db.units)}, rep=0)
                    group(db, it * 2 + 1, rep=1)

            ffn(0, 0)

            p = ph["qkv"]
            stat_post(1, p.group0)

            def gates(j):
                if j == 0:
                    pe.wait_ge(w_if_ready, 2)
                for c in (2 * j, 2 * j + 1):
                    ins = mm(PS[0:40, 6, 0:T], w_if[:, c, :], x[:, c, :], start=(c == 0), stop=(c == C - 1), skip_group_check=True)
                if j == C // 2 - 1:
                    ins.then_inc(gate_mm, 1)

            def turn_rows():
                pe.wait_ge(row_act, 3)
                for k0, src in ((0, c_row), (3 * H, gr_row)):
                    for t in range(3):
                        n = P if t < 2 else TS
                        turn(PS[0:n, 5, k0 + t * H:k0 + (t + 1) * H], src[:, t * P:t * P + n], ident[0:H, 0:H])
                turn(PS[:, 5, 6 * H:6 * H + B * H], n0_rows[:, :], ident[0:B * H, 0:B * H]).then_inc(row_turned, 1)

            def cell_top(h):
                pe.wait_ge(head_rows, h + 1)
                mm(PS[:, 6, 0:T + TS], ones[0:H, :], rows_h[:, 0:T + TS], start=True, stop=True, skip_group_check=True).then_inc(tables, 1)
                pe.wait_ge(banks_read, h + (ph["qkv"].group0 + 1))
                mm(PS[:, 7, 0:TP], kT[:, 0:P], qT[:, 0:TP], start=True, stop=True, skip_group_check=True)
                mm(PS[:, 7, TP:TP + P], kT[:, P:TP], qT[:, P:TP], start=False, stop=True, skip_group_check=True)
                mm(PS[0:TS, 7, 3 * P:3 * P + TS], kT[:, TP:T], qT[:, TP:T], start=False, stop=True, skip_group_check=True).then_inc(scores, 1)
                for t in range(2):
                    turn(PS[:, 4, t * P:(t + 1) * P], kT[:, t * P:(t + 1) * P], ident[:, :])
                    for i in range(2):
                        if t and i:
                            pe.wait_ge(qw_ready, h + 1)
                        turn(PS[:, 5, (2 * t + i) * P:(2 * t + i + 1) * P], vT[:, i, t * P:(t + 1) * P], ident[:, :])
                for i in range(2):
                    turn(PS[0:TS, 4, (2 + i) * P:(3 + i) * P], vT[:, i, TP:T], ident[:, :])
                turn(PS[0:TS, 6, T + TS:T + TS + P], kT[:, TP:T], ident[:, :]).then_inc(kv_turned, 1)

            def cell_num(h):
                pe.wait_ge(prob_ready, h + 1)
                pe.wait_ge(kw_seq_ready, h + 1)
                pe.wait_ge(v_ready, h + 1)
                pe.wait_ge(qn_ready, h + 1)
                pe.wait_ge(C0_in, h * 16 + 16)

                def intra(bank, lhs):
                    mm(PS[:, bank, 0:TP], lhs(0, P), prob[:, 0:TP], start=True, stop=False, skip_group_check=True)
                    mm(PS[:, bank, P:TP], lhs(1, P), prob[:, TP:TP + P], start=False, stop=False, skip_group_check=True)
                    mm(PS[:, bank, TP:T], lhs(2, TS), prob_s[:, :], start=False, stop=False, skip_group_check=True)

                for b in range(B):
                    ins = mm(PS[0:TS, 6, 0:DV], qw_seq[:, b, :], C0[:, b, :], start=(b == 0), stop=(b == B - 1),
                             skip_group_check=True)
                ins.then_inc(inter_done, 1)
                mm(PS[:, 7, 0:T], ones[0:H, :], rows_h[:, T + TS:2 * T + TS], start=True, stop=True, skip_group_check=True)
                half = lambda i: slice(i * P, (i + 1) * P)
                intra(4, lambda t, n: v_tok[0:n, t, half(0)])
                pe.wait_ge(inter_ready, h + 1)
                intra(6, lambda t, n: ones[0:n, :])
                mm(PS[:, 6, TP:T], ones[:, :], qn[:, :], start=False, stop=True, skip_group_check=True).then_inc(den_done, 1)
                intra(5, lambda t, n: v_tok[0:n, t, half(1)])
                for i in range(2):
                    ins = mm(PS[:, 4 + i, TP:T], inter[:, half(i)], ident[0:TS, 0:TS], start=False, stop=True,
                             skip_group_check=True)
                ins.then_inc(num_done, 1)

            def state_pair(h, pair):
                for i in range(2):
                    ins = mm(PS[:, 5 + 2 * (pair % 2), i * DV:(i + 1) * DV], kw_seq[:, 2 * pair + i, :], v_tok[0:TS, 2, :],
                             start=(i == 0), stop=True, skip_group_check=True)
                ins.then_inc(Cs_done, 1)

            def cell_norm(h):
                pe.wait_ge(hq_sq, h + 1)
                mm(PS[:, 6, 0:T], ones[:, :], sq[:, 0, 0, :], start=True, stop=False, skip_group_check=True)
                mm(PS[:, 6, 0:T], ones[:, :], sq[:, 0, 1, :], start=False, stop=True, skip_group_check=True).then_inc(hq_sum, 1)
                mm(PS[:, 4, 0:DV], kw[:, 0, :], v_tok[:, 0, :], start=True, stop=False, skip_group_check=True)
                mm(PS[:, 4, 0:DV], kw[:, 1, :], v_tok[:, 1, :], start=False, stop=True, skip_group_check=True)
                mm(PS[:, 4, DV:DV + B], kw[0:TS, 2, :], seg[:, :], start=False, stop=True, skip_group_check=True)
                mm(PS[:, 4, DV + B:DV + B + 1], kw[:, 0, :], ones[:, 0:1], start=False, stop=False, skip_group_check=True)
                mm(PS[:, 4, DV + B:DV + B + 1], kw[:, 1, :], ones[:, 0:1], start=False, stop=True, skip_group_check=True).then_inc(Cp_done, 1)
                state_pair(h, 0)
                state_pair(h, 1)

            def cell_state(h):
                pe.wait_ge(C_new, h * B + 2)
                state_pair(h, 2)
                pe.wait_ge(C_new, h * B + 4)
                state_pair(h, 3)

            def cell_before(h):
                return {1: [lambda: cell_top(h)], 4: [lambda: cell_num(h)], 6: [lambda: cell_norm(h)], 7: [lambda: cell_state(h)]}

            before = prep_windows("qkv", [lambda: gates(C // 2 - 1), lambda: stat_rx("qkv", p.group0)])
            for j in range(1, C // 2):
                before[j].insert(0, lambda j=j: gates(j - 1))
            group(p, 0, before, single=True)
            before = cell_before(0)
            before[3] = [turn_rows, lambda: pe.wait_ge(row_cols, 1)] + before.pop(1)
            group(p, 1, before, single=True)
            with pe.Fori(2, p.groups) as g:
                group(p, g, cell_before(g - 1), single=True)
            o = ph["o"]
            group(o, 0, cell_before(H - 1), single=True)
            pe.wait_ge(n_done, H)
            pe.wait_ge(C_new, H * B)
            turn(PS[0:B * H + H, 7, 0:P], n_new[:, :], ident[:, :]).then_inc(n_turned, 1)
            pe.wait_ge(n_copied, 1)
            with pe.Fori(1, o.groups) as g:
                group(o, g)
            p = ph["out"]
            phase(p, prep_windows("out"))
            ffn(1, 2)

            end = ph["down1b"].group0 + ph["down1b"].groups
            stat_post(3, end)
            for k in range(C // 4):
                pe.wait_ge(prep_front, C // 2 * prep_no["end"] + 2 * k + 2)
                for t in range(3):
                    i = 3 * k + t
                    n = P if t < 2 else TS
                    if i >= 8:
                        pe.wait_ge(y_copied, i - 7)
                    for c in range(4):
                        ins = turn(PS[0:n, i % 8, c * P:(c + 1) * P], x[:, 4 * k + c, t * P:t * P + n], ident[:, :])
                    ins.then_inc(y_turned, 1)


_INS = ["x_prompt", "x_sample", "cache_conv", "state_C", "state_n", "state_m", "conv_w_pw1", "conv_b_pw1",
        "conv_w_dw", "conv_b_dw", "conv_ln_g", "conv_ln_b", "conv_w_pw2", "conv_b_pw2", "mlstm_w_q", "mlstm_w_k",
        "mlstm_w_v", "mlstm_w_o", "mlstm_w_i", "mlstm_b_i", "mlstm_w_f", "mlstm_b_f", "mlstm_g_norm",
        "mlstm_w_out", "ffn_w_gate", "ffn_w_up", "ffn_w_down", "norm_mix_pre", "norm_mix_post", "norm_ffn_pre",
        "norm_ffn_post"]


def kernel(**inputs):
    import numpy as np
    import concourse.bacc as bacc
    from concourse.bass_utils import run_bass_kernel_spmd

    b, tp, d = inputs["x_prompt"].shape
    bs, ts, _ = inputs["x_sample"].shape
    nl, _, tail, _ = inputs["cache_conv"].shape
    nm, _, heads, dk, dv = inputs["state_C"].shape
    outs = [("y_prompt", (b, tp, d)), ("y_sample", (bs, ts, d)), ("conv_prompt", (nl, b, tail, d)),
            ("conv_sample", (nl, bs, tail, d)), ("C_prompt", (nm, b, heads, dk, dv)), ("n_prompt", (nm, b, heads, dk)),
            ("m_prompt", (nm, b, heads)), ("C_sample", (nm, bs, heads, dk, dv)), ("n_sample", (nm, bs, heads, dk)),
            ("m_sample", (nm, bs, heads))]
    nc = bacc.Bacc("TRN2", target_bir_lowering=False, num_devices=1, dynamic_dma_scratch_size=4096)
    arrays, args = {}, []
    for name in _INS:
        a = np.ascontiguousarray(inputs[name])
        arrays[f"in_{name}"] = a
        args.append(nc.dram_tensor(f"in_{name}", a.shape, mybir.dt.from_np(a.dtype), kind="ExternalInput").ap())
    for name, shape in outs:
        args.append(nc.dram_tensor(f"out_{name}", shape, F32, kind="ExternalOutput").ap())
    trunk_kernel(nc, *args)
    r = run_bass_kernel_spmd(nc, [arrays], core_ids=[0])
    return tuple(r.results[0][f"out_{name}"] for name, _ in outs)
```
